# Optimizing a Trainium2 kernel written in Bass

```python
import jax, jax.numpy as jnp
from jax import lax
import numpy as np

D_MODEL = 1024
BATCH = 1
SEQ = 256
DEPTH = 4

N_MIXERS = 3
N_SB = (DEPTH + 2) // 3
N_ML = (DEPTH + 1) // 3
N_MLA = DEPTH // 3

BLOCK_Q = 128
EPS = 1e-6

SB_HEADS = 16
SB_HEAD_DIM = D_MODEL // SB_HEADS

ML_HEADS = 8
ML_V_DIM = D_MODEL // ML_HEADS
ML_QK_DIM = ML_V_DIM // 2
ML_CHUNK = 64
ML_CONV = 4
ML_QK_COLS = 2 * ML_HEADS * ML_QK_DIM
ML_IN_COLS = ML_QK_COLS + 2 * D_MODEL + 2 * ML_HEADS

MLA_HEADS = 16
MLA_NOPE = 64
MLA_ROPE = 32
MLA_V = 64
MLA_Q_RANK = 384
MLA_KV_RANK = 256
MLA_IN_COLS = MLA_Q_RANK + MLA_KV_RANK + MLA_ROPE
ROPE_THETA = 10000.0

D_FF = 2816

kernel_name = 'interleaved_sb_mlstm_mla_macaron'

def rmsnorm(x, g):
    xf = x.astype(jnp.float32)
    y = xf * lax.rsqrt(jnp.mean(xf * xf, axis=-1, keepdims=True) + EPS)
    return (y * g.astype(jnp.float32)).astype(x.dtype)

def swiglu(x, wi, wo):
    gate, up = jnp.split(x @ wi, 2, axis=-1)
    return (jax.nn.silu(gate) * up) @ wo

def sweep_query_blocks(block_fn, q):
    B, H, S, d = q.shape
    nb = S // BLOCK_Q
    qb = q.reshape(B, H, nb, BLOCK_Q, d).transpose(2, 0, 1, 3, 4)
    starts = jnp.arange(nb, dtype=jnp.int32) * BLOCK_Q
    out = lax.map(lambda a: block_fn(a[0], a[1]), (qb, starts))
    return out.transpose(1, 2, 0, 3, 4).reshape(B, H, S, out.shape[-1])

def stick_breaking_attention(x, w_in, w_out):
    B, S, _ = x.shape
    q, k, v = jnp.split(x @ w_in, 3, axis=-1)
    to_heads = lambda t: t.reshape(B, S, SB_HEADS, SB_HEAD_DIM).transpose(0, 2, 1, 3)
    q, k, v = to_heads(q), to_heads(k), to_heads(v)
    scale = SB_HEAD_DIM ** -0.5
    key_pos = jnp.arange(S, dtype=jnp.int32)

    def block(qb, start):
        z = jnp.einsum('bhqd,bhkd->bhqk', qb, k, preferred_element_type=jnp.float32) * scale
        q_pos = start + jnp.arange(BLOCK_Q, dtype=jnp.int32)
        strict = key_pos[None, :] < q_pos[:, None]
        log_beta = jax.nn.log_sigmoid(z)
        log_fail = jnp.where(strict, jax.nn.log_sigmoid(-z), 0.0)
        between = lax.cumsum(log_fail, axis=3, reverse=True) - log_fail
        w = jnp.where(strict, jnp.exp(log_beta + between), 0.0)
        return jnp.einsum('bhqk,bhkd->bhqd', w.astype(v.dtype), v)

    o = sweep_query_blocks(block, q)
    return o.transpose(0, 2, 1, 3).reshape(B, S, D_MODEL) @ w_out

def causal_depthwise_conv(x, w):
    K, C = w.shape
    return lax.conv_general_dilated(x, w[:, None, :].astype(x.dtype), window_strides=(1,),
                                    padding=[(K - 1, 0)],
                                    dimension_numbers=('NWC', 'WIO', 'NWC'),
                                    feature_group_count=C)

def mlstm(x, w_in, conv_w, b_igate, b_fgate, head_gain, w_out):
    B, S, _ = x.shape
    H, dk, dv, L = ML_HEADS, ML_QK_DIM, ML_V_DIM, ML_CHUNK
    f32 = jnp.float32
    p = x @ w_in
    qk, v, o_pre, gates = jnp.split(p, [ML_QK_COLS, ML_QK_COLS + D_MODEL, ML_QK_COLS + 2 * D_MODEL], axis=-1)
    qk = jax.nn.silu(causal_depthwise_conv(qk, conv_w))
    q, k = jnp.split(qk, 2, axis=-1)
    i_pre, f_pre = jnp.split(gates, 2, axis=-1)
    log_i = (i_pre + b_igate).astype(f32)
    log_f = jax.nn.log_sigmoid((f_pre + b_fgate).astype(f32))
    nc = S // L

    def chunks(t, d):
        return t.astype(f32).reshape(B, nc, L, H, d).transpose(1, 0, 3, 2, 4)

    qc = chunks(q * (dk ** -0.5), dk)
    kc = chunks(k, dk)
    vc = chunks(v, dv)
    lic = log_i.reshape(B, nc, L, H).transpose(1, 0, 3, 2)
    lfc = log_f.reshape(B, nc, L, H).transpose(1, 0, 3, 2)
    causal = jnp.tril(jnp.ones((L, L), dtype=bool))

    def step(carry, inp):
        C, n, m = carry
        qb, kb, vb, li, lf = inp
        b = jnp.cumsum(lf, axis=-1)
        dmat = jnp.where(causal, b[..., :, None] - b[..., None, :] + li[..., None, :], -jnp.inf)
        inter = b + m[..., None]
        m_t = jnp.maximum(jnp.max(dmat, axis=-1), inter)
        wt = jnp.exp(dmat - m_t[..., None])
        a = jnp.exp(inter - m_t)
        s = jnp.einsum('bhtd,bhsd->bhts', qb, kb) * wt
        num = jnp.einsum('bhts,bhsv->bhtv', s, vb) + a[..., None] * jnp.einsum('bhtd,bhdv->bhtv', qb, C)
        den = jnp.sum(s, axis=-1) + a * jnp.einsum('bhtd,bhd->bht', qb, n)
        h = num / jnp.maximum(jnp.abs(den), jnp.exp(-m_t))[..., None]
        b_last = b[..., -1]
        g = b_last[..., None] - b + li
        m_new = jnp.maximum(b_last + m, jnp.max(g, axis=-1))
        decay = jnp.exp(b_last + m - m_new)
        wk = jnp.exp(g - m_new[..., None])
        C_new = decay[..., None, None] * C + jnp.einsum('bhs,bhsd,bhsv->bhdv', wk, kb, vb)
        n_new = decay[..., None] * n + jnp.einsum('bhs,bhsd->bhd', wk, kb)
        return (C_new, n_new, m_new), h

    init = (jnp.zeros((B, H, dk, dv), f32), jnp.zeros((B, H, dk), f32), jnp.zeros((B, H), f32))
    _, hs = lax.scan(step, init, (qc, kc, vc, lic, lfc))
    h = hs.transpose(1, 0, 3, 2, 4).reshape(B, S, H, dv)
    h = rmsnorm(h, head_gain).reshape(B, S, D_MODEL).astype(x.dtype)
    return (jax.nn.sigmoid(o_pre) * h) @ w_out

def apply_rope(t, positions):
    half = t.shape[-1] // 2
    inv = ROPE_THETA ** (-jnp.arange(half, dtype=jnp.float32) / half)
    ang = positions.astype(jnp.float32)[:, :, None, None] * inv
    cos, sin = jnp.cos(ang), jnp.sin(ang)
    t1, t2 = jnp.split(t.astype(jnp.float32), 2, axis=-1)
    return jnp.concatenate([t1 * cos - t2 * sin, t1 * sin + t2 * cos], axis=-1).astype(t.dtype)

def mla(x, positions, w_in, g_q, w_uq, g_kv, w_ukv, w_out):
    B, S, _ = x.shape
    H = MLA_HEADS
    c_q, c_kv, k_r = jnp.split(x @ w_in, [MLA_Q_RANK, MLA_Q_RANK + MLA_KV_RANK], axis=-1)
    qh = (rmsnorm(c_q, g_q) @ w_uq).reshape(B, S, H, MLA_NOPE + MLA_ROPE)
    q_nope, q_rope = jnp.split(qh, [MLA_NOPE], axis=-1)
    q = jnp.concatenate([q_nope, apply_rope(q_rope, positions)], axis=-1)
    kvh = (rmsnorm(c_kv, g_kv) @ w_ukv).reshape(B, S, H, MLA_NOPE + MLA_V)
    k_nope, v = jnp.split(kvh, [MLA_NOPE], axis=-1)
    k_rope = apply_rope(k_r[:, :, None, :], positions)
    k = jnp.concatenate([k_nope, jnp.broadcast_to(k_rope, (B, S, H, MLA_ROPE))], axis=-1)
    q, k, v = (t.transpose(0, 2, 1, 3) for t in (q, k, v))
    scale = (MLA_NOPE + MLA_ROPE) ** -0.5
    key_pos = jnp.arange(S, dtype=jnp.int32)

    def block(qb, start):
        s = jnp.einsum('bhqd,bhkd->bhqk', qb, k, preferred_element_type=jnp.float32) * scale
        q_pos = start + jnp.arange(BLOCK_Q, dtype=jnp.int32)
        s = jnp.where(key_pos[None, :] <= q_pos[:, None], s, -jnp.inf)
        p = jax.nn.softmax(s, axis=-1)
        return jnp.einsum('bhqk,bhkd->bhqd', p.astype(v.dtype), v)

    o = sweep_query_blocks(block, q)
    return o.transpose(0, 2, 1, 3).reshape(B, S, H * MLA_V) @ w_out

def setup_inputs(seed: int = 0) -> dict:
    key = jax.random.key(seed)
    ks = iter(jax.random.split(key, 32))
    D = D_MODEL

    def w(shape, fan_in):
        return jax.random.normal(next(ks), shape, jnp.float32) * (fan_in ** -0.5)

    def gain(shape):
        return 1.0 + 0.01 * jax.random.normal(next(ks), shape, jnp.float32)

    x = jax.random.normal(next(ks), (BATCH, SEQ, D), jnp.float32)
    positions = jnp.broadcast_to(jnp.arange(SEQ, dtype=jnp.int32)[None, :], (BATCH, SEQ))
    return {
        'x': x,
        'positions': positions,
        'ln_ffn1': gain((DEPTH, D)),
        'ffn1_wi': w((DEPTH, D, 2 * D_FF), D),
        'ffn1_wo': w((DEPTH, D_FF, D), D_FF),
        'ln_mix': gain((DEPTH, D)),
        'ln_ffn2': gain((DEPTH, D)),
        'ffn2_wi': w((DEPTH, D, 2 * D_FF), D),
        'ffn2_wo': w((DEPTH, D_FF, D), D_FF),
        'sb_w_in': w((N_SB, D, 3 * D), D),
        'sb_w_out': w((N_SB, D, D), D),
        'ml_w_in': w((N_ML, D, ML_IN_COLS), D),
        'ml_conv_w': w((N_ML, ML_CONV, ML_QK_COLS), ML_CONV),
        'ml_b_igate': 0.1 * jax.random.normal(next(ks), (N_ML, ML_HEADS), jnp.float32),
        'ml_b_fgate': jnp.linspace(3.0, 6.0, ML_HEADS, dtype=jnp.float32)[None, :]
                      + 0.1 * jax.random.normal(next(ks), (N_ML, ML_HEADS), jnp.float32),
        'ml_head_gain': gain((N_ML, ML_HEADS, ML_V_DIM)),
        'ml_w_out': w((N_ML, D, D), D),
        'mla_w_in': w((N_MLA, D, MLA_IN_COLS), D),
        'mla_g_q': gain((N_MLA, MLA_Q_RANK)),
        'mla_w_uq': w((N_MLA, MLA_Q_RANK, MLA_HEADS * (MLA_NOPE + MLA_ROPE)), MLA_Q_RANK),
        'mla_g_kv': gain((N_MLA, MLA_KV_RANK)),
        'mla_w_ukv': w((N_MLA, MLA_KV_RANK, MLA_HEADS * (MLA_NOPE + MLA_V)), MLA_KV_RANK),
        'mla_w_out': w((N_MLA, MLA_HEADS * MLA_V, D), MLA_HEADS * MLA_V),
        'ln_final': gain((D,)),
    }

def reference(x, positions, ln_ffn1, ffn1_wi, ffn1_wo, ln_mix, ln_ffn2, ffn2_wi, ffn2_wo,
              sb_w_in, sb_w_out,
              ml_w_in, ml_conv_w, ml_b_igate, ml_b_fgate, ml_head_gain, ml_w_out,
              mla_w_in, mla_g_q, mla_w_uq, mla_g_kv, mla_w_ukv, mla_w_out,
              ln_final):
    h = x
    for i in range(DEPTH):
        h = h + 0.5 * swiglu(rmsnorm(h, ln_ffn1[i]), ffn1_wi[i], ffn1_wo[i])
        u = rmsnorm(h, ln_mix[i])
        j = i // N_MIXERS
        kind = i % N_MIXERS
        if kind == 0:
            mix = stick_breaking_attention(u, sb_w_in[j], sb_w_out[j])
        elif kind == 1:
            mix = mlstm(u, ml_w_in[j], ml_conv_w[j], ml_b_igate[j], ml_b_fgate[j],
                        ml_head_gain[j], ml_w_out[j])
        else:
            mix = mla(u, positions, mla_w_in[j], mla_g_q[j], mla_w_uq[j], mla_g_kv[j],
                      mla_w_ukv[j], mla_w_out[j])
        h = h + mix
        h = h + 0.5 * swiglu(rmsnorm(h, ln_ffn2[i]), ffn2_wi[i], ffn2_wo[i])
    return rmsnorm(h, ln_final)


_drawn_inputs = setup_inputs


def setup_inputs(seed=0):
    import zlib

    import numpy as np

    out = dict(_drawn_inputs(seed))
    spreads = {}
    factors = {'ln_ffn1': 6.359,
     'ln_mix': 4.24,
     'ln_ffn2': 7.535,
     'ml_b_igate': 64.0,
     'ml_head_gain': 64.0,
     'mla_g_q': 31.171,
     'mla_g_kv': 29.129,
     'ln_final': 31.772}
    for name, (base, spread) in spreads.items():
        noise = np.random.default_rng([zlib.crc32(name.encode()), seed]).standard_normal(out[name].shape)
        drawn = base * np.exp(spread * noise) if base else spread * noise
        out[name] = __import__('jax').numpy.asarray(drawn.astype(out[name].dtype))
    for name, factor in factors.items():
        out[name] = (out[name] * factor).astype(out[name].dtype)
    return out
```

```python
from contextlib import ExitStack

import concourse.bass as bass
from concourse import mybir

F32 = mybir.dt.float32
F32R = mybir.dt.float32r
BF16 = mybir.dt.bfloat16
I32 = mybir.dt.int32
ACT = mybir.ActivationFunctionType
ALU = mybir.AluOpType
AX = mybir.AxisListType.X

P = 128
SEQ = 256
TT = SEQ // P
D = 1024
KD = D // P
NCOL = 512
HALVES = D // NCOL
EPS = 1e-6
DEPTH = 4
D_FF = 2816
FC = 256
CHUNKS = D_FF // FC
RING = 3
PCOLS = 2048
MIX_COLS = 16704
NEG = -1e30

SB_HEADS = 16
SB_SCALE = 64 ** -0.5
ML_HEADS = 8
ML_SCALE = 64 ** -0.5
MLA_HEADS = 16
NOPE, ROPE, VD = 64, 32, 64
QK = NOPE + ROPE
HALF = ROPE // 2
Q_RANK, KV_RANK = 384, 256
MLA_IN = Q_RANK + KV_RANK + ROPE
MLA_SCALE = QK ** -0.5
ROPE_THETA = 10000.0
TWO_PI = 6.283185307179586
TWO_PI_PARTS = (6.28125, 0.0019350051879882812, 3.019916050561733e-07)
ROUND = 1.5 * 2.0 ** 23
SIN_MAX = 3.1415925
GROUP = 4
GROUPS = [(t, nh) for t in range(TT) for nh in range(HALVES)]
UP = ((0, 1), (4, 5))
OWN = 1000

GAIN_FFN1, GAIN_MIX, GAIN_FFN2 = 0, DEPTH * KD, 2 * DEPTH * KD
GAIN_Q, GAIN_KV, GAIN_HEAD, CONV_W = 0, 3, 5, 13
N_GAINS_1 = 3 * DEPTH * KD
N_GAINS_2 = CONV_W + 4 * KD


def halves(n):
    return (0, n // 2), (n // 2, n)


class Sub:
    pass


class Piece:

    def __init__(self, tiles, cols, gain, sources):
        self.tiles, self.cols, self.gain, self.sources = tiles, cols, gain, sources


def rows_piece(w, k0, tiles, c0, cols, gain):
    v = w.rearrange("(k p) n -> p k n", p=P)
    if tiles > 1:
        cut = [(a, b, 0, cols) for a, b in ((0, tiles // 2), (tiles // 2, tiles))]
    else:
        cut = [(0, 1, a, b) for a, b in halves(cols)]
    return Piece(tiles, cols, gain,
                 [(a, b, ca, cb, v[:, k0 + a:k0 + b, c0 + ca:c0 + cb]) for a, b, ca, cb in cut])


def up_piece(wi, c, part, gain):
    v = wi.rearrange("(k p) (s n) -> p k s n", p=P, s=2)
    return Piece(4, 2 * FC, gain,
                 [(0, 4, s * FC, (s + 1) * FC, v[:, 4 * part:4 * part + 4, s, bass.ds(c * FC, FC)])
                  for s in range(2)])


def down_piece(wo, c):
    return Piece(2, D, None,
                 [(j, j + 1, 0, D, wo[bass.ds(c * FC + j * P, P), :].rearrange("(k p) n -> p k n", k=1))
                  for j in range(2)])


def trunk(nc, x, positions, ln_ffn1, ffn1_wi, ffn1_wo, ln_mix, ln_ffn2, ffn2_wi, ffn2_wo,
          sb_w_in, sb_w_out, ml_w_in, ml_conv_w, ml_b_igate, ml_b_fgate, ml_head_gain, ml_w_out,
          mla_w_in, mla_g_q, mla_w_uq, mla_g_kv, mla_w_ukv, mla_w_out, ln_final, out):
    ctx = ExitStack()
    with ctx:
        def sb(name, shape, dt=F32):
            return ctx.enter_context(nc.sbuf_tensor(name, shape, dt))

        def sem(name):
            return ctx.enter_context(nc.semaphore(name))

        raw = sb("raw", [P, RING, PCOLS])
        whi = sb("whi", [P, RING, PCOLS], F32R)
        wlo = sb("wlo", [P, RING, PCOLS], F32R)
        h = sb("h", [P, TT, D])
        xT_hi = sb("xT_hi", [P, KD, SEQ], F32R)
        xT_lo = sb("xT_lo", [P, KD, SEQ], F32R)
        hid = sb("hid", [P, TT, FC])
        silu = sb("silu", [P, TT, FC])
        hidT_hi = sb("hidT_hi", [P, FC // P, SEQ], F32R)
        hidT_lo = sb("hidT_lo", [P, FC // P, SEQ], F32R)
        y = sb("y", [P, TT, D])
        gains1 = sb("gains1", [P, N_GAINS_1])
        gains2 = sb("gains2", [P, N_GAINS_2])
        ident = sb("ident", [P, P])
        ident_b = sb("ident_b", [P, P], BF16)
        neg_tri = sb("neg_tri", [P, P])
        neg_ones = sb("neg_ones", [P, P])
        ones = sb("ones", [P, 2])
        mask = sb("mask", [P, 6, NCOL], BF16)
        ssq = sb("ssq", [P, TT])
        mean_sq = sb("mean_sq", [P, TT])
        rstd = sb("rstd", [P, TT])
        minus_half = sb("minus_half", [P, 16])
        gate_bias = sb("gate_bias", [ML_HEADS, 2])
        pos_i = sb("pos_i", [P, TT], I32)
        mix = sb("mix", [P, MIX_COLS])
        psum = ctx.enter_context(nc.psum_tensor("psum", [P, 8, NCOL], F32))

        def carve(start, *dims):
            n = 1
            for d in dims:
                n *= d
            assert start + n <= MIX_COLS, (start, n)
            v = mix[:, start:start + n]
            if len(dims) == 2:
                v = v.rearrange("p (a b) -> p a b", a=dims[0])
            if len(dims) == 3:
                v = v.rearrange("p (a b c) -> p a b c", a=dims[0], b=dims[1])
            return v, start + n

        stage, at0 = carve(0, TT, NCOL)
        qT, at = carve(at0, KD, SEQ)
        kT_even, at = carve(at, KD, SEQ)
        kT_odd, at = carve(at, KD, SEQ)
        v_sb, at = carve(at, TT, D)
        sb_e, at = carve(at, 2, 3 * NCOL)
        sb_sp, at = carve(at, 2, 3 * NCOL)
        mqT, at = carve(at0, 4, SEQ)
        mkT_even, at = carve(at, 4, SEQ)
        mkT_odd, at = carve(at, 4, SEQ)
        mv, at = carve(at, TT, D)
        mo, at = carve(at, TT, D)
        g_rows, at = carve(at, 9, SEQ)
        g_i, g_f, g_t, g_F, g_a, g_em, g_one, g_min = (g_rows[0:ML_HEADS, j, :] for j in range(8))
        g_M = g_rows[:, 8, :]
        gate_in, at = carve(at, TT, 16)
        gate_T, at = carve(at, 4, ML_HEADS)
        den, at = carve(at, TT, GROUP)
        mssq, at = carve(at, TT, ML_HEADS)
        mrms, at = carve(at, TT, ML_HEADS)
        sel, at = carve(at, ML_HEADS, P)
        conv_in, atc = carve(at, KD, 3 + SEQ)
        conv_out, atd = carve(atc, KD, SEQ)
        ml_wt = mix[:, at:at + 3 * NCOL]
        ml_sw = mix[:, atc:atc + 3 * NCOL]
        ml_sq = mix[:, atc:atc + TT * D].rearrange("p (t n) -> p t n", t=TT)
        lqT, at = carve(at0, MLA_HEADS, SEQ)
        lkT, at = carve(at, MLA_HEADS, SEQ)
        lv, at = carve(at, TT, D)
        lq, at = carve(at, TT * GROUP, QK)
        lk, at = carve(at, TT * GROUP, QK)
        angle, at = carve(at, 4, HALF)
        turns, at = carve(at, 4, HALF)
        trig, at = carve(at, 4, HALF)
        inv_freq, at = carve(at, HALF)
        kr, at = carve(at, TT, ROPE)
        rope_tmp, at = carve(at, 4, TT * GROUP, HALF)
        pos_f, at = carve(at, TT)
        lssq, at = carve(at, 2, TT)
        lms, at = carve(at, 2, TT)
        lrms, at = carve(at, 2, TT)
        lmax, at = carve(at, 8)
        lsum, at = carve(at, 8)
        lc, _ = carve(at, TT, MLA_IN)
        l_px, at = carve(at, 3 * NCOL)
        l_pT, at = carve(at, 3 * NCOL)
        gain_row, _ = carve(0, D)

        raw_loaded = [sem(f"raw_loaded{j}") for j in range(RING)]
        hi_ready = sem("hi_ready")
        lo_ready = sem("lo_ready")
        piece_used = sem("piece_used")
        proj_done = sem("proj_done")
        proj_read = sem("proj_read")
        silu_done = sem("silu_done")
        tr_done = sem("tr_done")
        tr_hi = sem("tr_hi")
        tr_read = sem("tr_read")
        acc_done = sem("acc_done")
        h_done = sem("h_done")
        ssq_done = sem("ssq_done")
        rstd_done = sem("rstd_done")
        x_loaded = sem("x_loaded")
        par_loaded = sem("par_loaded")
        const_done = sem("const_done")
        par_T = sem("par_T")
        gains_ready = sem("gains_ready")
        y_ready = sem("y_ready")
        plain_T = sem("plain_T")
        plain_read = sem("plain_read")
        pad_ready = sem("pad_ready")
        z_done = sem("z_done")
        abs_done = sem("abs_done")
        exp_done = sem("exp_done")
        ln_done = sem("ln_done")
        sp_done = sem("sp_done")
        r_done = sem("r_done")
        w_done = sem("w_done")
        av_done = sem("av_done")
        gate_T_done = sem("gate_T_done")
        gate_abs = sem("gate_abs")
        gate_ln = sem("gate_ln")
        gate_m = sem("gate_m")
        gate_em = sem("gate_em")
        gate_back = sem("gate_back")
        gate_cols = sem("gate_cols")
        conv_done = sem("conv_done")
        mqk_ready = sem("mqk_ready")
        mo_ready = sem("mo_ready")
        s_done = sem("s_done")
        lw_done = sem("lw_done")
        wt_done = sem("wt_done")
        sw_done = sem("sw_done")
        num_done = sem("num_done")
        num_read = sem("num_read")
        msq_done = sem("msq_done")
        mssq_done = sem("mssq_done")
        mrms_done = sem("mrms_done")
        lssq_done = sem("lssq_done")
        lrms_done = sem("lrms_done")
        angle_done = sem("angle_done")
        trig_done = sem("trig_done")
        lstage_ready = sem("lstage_ready")
        sc_done = sem("sc_done")
        sub_done = sem("sub_done")
        px_done = sem("px_done")
        pT_done = sem("pT_done")
        pT_read = sem("pT_read")
        lav_done = sem("lav_done")
        dve_chain = sem("dve_chain")
        act_chain = sem("act_chain")
        pool_chain = sem("pool_chain")
        final_done = sem("final_done")
        gainrow_loaded = sem("gainrow_loaded")
        out_stored = sem("out_stored")

        subs, static = [], {}
        pieces, blocks, fills, plains, ffns, sbs, ys = 0, 0, TT * HALVES, 0, 0, 0, 0
        for i in range(DEPTH):
            for part in range(3):
                s = Sub()
                s.index, s.piece0, s.block0, s.fill0, s.plain0, s.y0 = len(subs), pieces, blocks, fills, plains, ys
                if part != 1:
                    s.kind, s.ffn = "ffn", ffns
                    s.wi, s.wo = (ffn1_wi[i], ffn1_wo[i]) if part == 0 else (ffn2_wi[i], ffn2_wo[i])
                    s.gain = (GAIN_FFN1 if part == 0 else GAIN_FFN2) + i * KD
                    s.n_pieces, s.n_blocks, s.n_fills, s.n_plain = 3 * CHUNKS, CHUNKS, CHUNKS + 4, 0
                    ffns += 1
                else:
                    s.kind, j = ("sb", "ml", "mla")[i % 3], i // 3
                    gain = GAIN_MIX + i * KD
                    if s.kind == "sb":
                        cols = [D, D + NCOL, 0, NCOL, 2 * D, 2 * D + NCOL]
                        ps = [rows_piece(sb_w_in[j], 4 * a, 4, c, NCOL, gain + 4 * a) for c in cols for a in range(2)]
                        s.n_blocks, s.n_plain, s.n_fills = 6, 8, 8
                        w_out, head_gain, s.inst = sb_w_out[j], None, sbs
                        sbs += 1
                    elif s.kind == "ml":
                        ps = [rows_piece(ml_w_in[j], 0, KD, 3 * D, 16, gain)]
                        ps += [rows_piece(ml_w_in[j], 4 * a, 4, b * NCOL, NCOL, gain + 4 * a)
                               for b in range(6) for a in range(2)]
                        s.n_blocks, s.n_plain, s.n_fills = 7, 4, 8
                        w_out, head_gain = ml_w_out[j], GAIN_HEAD
                    else:
                        ps = [rows_piece(mla_w_in[j], 4 * a, 4, 0, NCOL, gain + 4 * a) for a in range(2)]
                        ps += [rows_piece(mla_w_in[j], 0, KD, NCOL, MLA_IN - NCOL, gain)]
                        ps += [rows_piece(mla_w_uq[j], 0, 3, b * GROUP * QK, GROUP * QK, OWN + GAIN_Q) for b in range(4)]
                        ps += [rows_piece(mla_w_ukv[j], 0, 2, b * NCOL, NCOL, OWN + GAIN_KV) for b in range(4)]
                        s.n_blocks, s.n_plain, s.n_fills = 10, 16, 11
                        w_out, head_gain = mla_w_out[j], None
                    s.out0 = pieces + len(ps)
                    ps += [rows_piece(w_out, 2 * a, 2, 0, D, None if head_gain is None else OWN + head_gain + 2 * a)
                           for a in range(4)]
                    s.n_pieces = len(ps)
                    static.update({pieces + n: p for n, p in enumerate(ps)})
                    ys += 4
                pieces += s.n_pieces
                blocks += s.n_blocks
                fills += s.n_fills
                plains += s.n_plain
                s.norm_fill0 = fills - 4
                subs.append(s)
        n_pieces = pieces
        for n, s in enumerate(s for s in subs if s.kind != "ffn"):
            s.pads = n + 1

        def gain_col(g):
            return gains2[:, g - OWN:g - OWN + 1] if g >= OWN else gains1[:, g:g + 1]

        def ffn_piece(s, role, c):
            if role == "C":
                return down_piece(s.wo, c)
            part = "AB".index(role)
            return up_piece(s.wi, c, part, s.gain + 4 * part)

        def piece_at(n):
            s = [s for s in subs if s.piece0 <= n][-1]
            if s.kind != "ffn":
                return static[n]
            m = n - s.piece0
            if m < 2:
                return ffn_piece(s, "AB"[m], 0)
            if m == s.n_pieces - 1:
                return ffn_piece(s, "C", CHUNKS - 1)
            c, r = (m + 1) // 3, (m + 1) % 3
            return ffn_piece(s, "ABC"[r], c if r < 2 else c - 1)

        def load(sp, p, m, c=0):
            slot = m % RING
            if not isinstance(c, int) or m + 3 * c >= RING:
                sp.wait_ge(lo_ready, m + 3 * c - (RING - 1))
            for a, b, ca, cb, src in p.sources:
                dst = raw[:, slot, 0:p.tiles * p.cols].rearrange("p (k n) -> p k n", k=p.tiles)[:, a:b, ca:cb]
                sp.dma_start(dst, src).then_inc(raw_loaded[slot], 16)

        def convert_act(act, p, m, c=0):
            slot = m % RING
            act.wait_ge(raw_loaded[slot], 32 * (m // RING + 1) + 32 * c)
            if not isinstance(c, int) or m + 3 * c >= RING:
                act.wait_ge(piece_used, m + 3 * c - (RING - 1))
            if p.gain is None:
                w = p.tiles * p.cols
                act.activation(whi[:, slot, 0:w], raw[:, slot, 0:w], ACT.Copy).then_inc(hi_ready, 1)
                return
            for k in range(p.tiles):
                r = slice(k * p.cols, (k + 1) * p.cols)
                last = act.activation(whi[:, slot, r], raw[:, slot, r], ACT.Copy, scale=gain_col(p.gain + k))
            last.then_inc(hi_ready, 1)

        def convert_dve(dve, p, m, c=0):
            slot = m % RING
            dve.wait_ge(hi_ready, m + 3 * c + 1)
            hi = whi[:, slot, :].bitcast(F32)
            if p.gain is None:
                w = p.tiles * p.cols
                dve.tensor_tensor(wlo[:, slot, 0:w], raw[:, slot, 0:w], hi[:, 0:w], ALU.subtract).then_inc(lo_ready, 1)
                return
            for k in range(p.tiles):
                r = slice(k * p.cols, (k + 1) * p.cols)
                last = dve.scalar_tensor_tensor(wlo[:, slot, r], raw[:, slot, r], gain_col(p.gain + k), hi[:, r],
                                                op0=ALU.mult, op1=ALU.subtract)
            last.then_inc(lo_ready, 1)

        def converts(eng, convert, *positions):
            for n in positions:
                if n < n_pieces:
                    convert(eng, piece_at(n), n)

        def passes(pe, dst, xh, xl, slot, cols, first, last):
            for n, (a, b) in enumerate(((xh, whi), (xh, wlo), (xl, whi))):
                m = pe.matmul(dst, a, b[:, slot, cols], start=first and n == 0, stop=last and n == 2)
            return m

        def project(pe, slot, t, bank, k0, tiles, cols, first, last):
            for k in range(tiles):
                m = passes(pe, psum[:, bank, 0:cols], xT_hi[:, k0 + k, t * P:(t + 1) * P],
                           xT_lo[:, k0 + k, t * P:(t + 1) * P], slot, slice(k * cols, (k + 1) * cols),
                           first and k == 0, last and k == tiles - 1)
            return m

        def out_group(pe, slot, g, xh, xl, k0, first, last):
            t, nh = GROUPS[g]
            for k in range(2):
                m = passes(pe, psum[:, g, :], xh[:, k0 + k, t * P:(t + 1) * P], xl[:, k0 + k, t * P:(t + 1) * P],
                           slot, slice(k * D + nh * NCOL, k * D + (nh + 1) * NCOL), first and k == 0, last and k == 1)
            return m

        def split_act(act, q, src, dst_hi):
            act.wait_ge(tr_done, q + 1)
            act.activation(dst_hi, src, ACT.Copy).then_inc(tr_hi, 1)

        def split_dve(dve, q, src, dst_hi, dst_lo):
            dve.wait_ge(tr_hi, q + 1)
            dve.tensor_tensor(dst_lo, src, dst_hi.bitcast(F32), ALU.subtract).then_inc(tr_read, 1)

        def fill_pe(pe, src, bank, t, nh):
            for j in range(4):
                m = pe.transpose(psum[:, bank, j * P:(j + 1) * P],
                                 src[:, t, nh * NCOL + j * P:nh * NCOL + (j + 1) * P], ident[:, :])
            m.then_inc(tr_done, 1)

        def fill_split(eng, q, bank, t, k0):
            src = psum[:, bank, :].rearrange("p (j n) -> p j n", j=4)
            hi, lo = (v[:, k0:k0 + 4, t * P:(t + 1) * P] for v in (xT_hi, xT_lo))
            if eng is nc.scalar:
                split_act(eng, q, src, hi)
            else:
                split_dve(eng, q, src, hi, lo)

        def norm_fill0(j):
            return 0 if j == 0 else subs[j - 1].norm_fill0

        def norm_fill(pe, j, g):
            q = norm_fill0(j) + g
            if j:
                pe.wait_ge(h_done, 4 * (j - 1) + g + 1)
            else:
                pe.wait_ge(x_loaded, 16 * TT)
            if q >= 2:
                pe.wait_ge(tr_read, q - 1)
            fill_pe(pe, h, 7 - g % 2, *GROUPS[g])

        def norm_split(eng, j, g):
            t, nh = GROUPS[g]
            fill_split(eng, norm_fill0(j) + g, 7 - g % 2, t, 4 * nh)

        def norm_act(act, j):
            for g in range(4):
                norm_split(act, j, g)
                if g >= 2:
                    t = g - 2
                    if j:
                        act.wait_ge(h_done, 4 * (j - 1) + 2 * t + 2)
                    act.activation(y[:, t, :], h[:, t, :], ACT.Square, accum_out=ssq[:, t:t + 1]).then_inc(ssq_done, 1)

        def norm_dve(dve, j, scale):
            def residual(g):
                t, nh = GROUPS[g]
                if g < 3:
                    dve.wait_ge(acc_done, 3 * (j - 1) + g + 1)
                else:
                    dve.wait_ge(piece_used, subs[j - 1].piece0 + subs[j - 1].n_pieces)
                hs = h[:, t, nh * NCOL:(nh + 1) * NCOL]
                dve.scalar_tensor_tensor(hs, psum[:, g, :], scale, hs, op0=ALU.mult, op1=ALU.add).then_inc(h_done, 1)

            if j:
                residual(0)
                residual(1)
                residual(2)
            if j == len(subs):
                residual(3)
                return
            norm_split(dve, j, 0)
            if j:
                residual(3)
            for g in (1, 2, 3):
                norm_split(dve, j, g)

        def first_piece(pe, j):
            s, q = subs[j], norm_fill0(j)
            p = piece_at(s.piece0)
            slot = s.piece0 % RING
            whole = p.tiles == KD
            norm_fill(pe, j, 1)
            norm_fill(pe, j, 2)
            pe.wait_ge(lo_ready, s.piece0 + 1)
            for t in range(TT):
                if t:
                    norm_fill(pe, j, 3)
                pe.wait_ge(tr_read, q + 2 * t + (2 if whole else 1))
                m = project(pe, slot, t, UP[0][t], 0, p.tiles, p.cols, True, whole)
                if whole and t == 0:
                    m.then_inc(proj_done, 1)
            m.then_inc(piece_used, 1)

        def last_piece(pe, s, n, xh, xl, k0):
            j = s.index + 1
            pe.wait_ge(lo_ready, n + 1)
            for g in range(4):
                m = out_group(pe, n % RING, g, xh, xl, k0, False, True)
                m.then_inc(acc_done if g < 3 else piece_used, 1)
                if g == 2 and j < len(subs):
                    norm_fill(pe, j, 0)
            if j < len(subs):
                first_piece(pe, j)

        def ffn_pe(pe, s):
            n0, b0, f0 = s.piece0, s.block0, s.fill0

            def up(m, c, part, banks):
                pe.wait_ge(lo_ready, m + 3 * c + 1)
                for t in range(TT):
                    i = project(pe, m % RING, t, banks[t], 4 * part, 4, 2 * FC, part == 0, part == 1)
                    if part and t == 0:
                        i.then_inc(proj_done, 1)
                i.then_inc(piece_used, 1)

            def hid_fill(c, q):
                pe.wait_ge(proj_read, 2 * (b0 + 1) + 2 * c)
                pe.wait_ge(tr_read, q)
                for b in range(FC // P):
                    for t in range(TT):
                        i = pe.transpose(psum[:, 6, (b * TT + t) * P:(b * TT + t + 1) * P],
                                         hid[:, t, b * P:(b + 1) * P], ident[:, :])
                i.then_inc(tr_done, 1)

            def chunk(c):
                if not (isinstance(c, int) and c == 1):
                    pe.wait_ge(proj_read, 2 * b0 + 2 * c)
                up(n0 - 1, c, 0, UP[1])
                hid_fill(c - 1, f0 + c - 1)
                up(n0, c, 1, UP[1])
                m = n0 + 1
                pe.wait_ge(lo_ready, m + 3 * c + 1)
                pe.wait_ge(tr_read, f0 + c)
                for g in range(4):
                    i = out_group(pe, m % RING, g, hidT_hi, hidT_lo, 0, isinstance(c, int) and c == 1, False)
                i.then_inc(piece_used, 1)

            pe.wait_ge(tr_read, norm_fill0(s.index) + 4)
            up(n0 + 1, 0, 1, UP[0])
            chunk(1)
            with pe.Fori(2, CHUNKS - 1) as c:
                chunk(c)
            chunk(CHUNKS - 1)
            hid_fill(CHUNKS - 1, f0 + CHUNKS - 1)
            pe.wait_ge(tr_read, f0 + CHUNKS)
            last_piece(pe, s, n0 + 3 * CHUNKS - 1, hidT_hi, hidT_lo, 0)

        def hidT_views(part):
            return part[:, :, :].rearrange("p b n -> p (b n)")

        def ffn_act(act, s):
            n0, b0 = s.piece0, s.block0

            def gate(c, banks):
                for t in range(TT):
                    if t == 0:
                        act.wait_ge(proj_done, b0 + 1 + c)
                    else:
                        act.wait_ge(piece_used, n0 + 2 if isinstance(c, int) and c == 0 else n0 + 1 + 3 * c)
                    act.activation(silu[:, t, :], psum[:, banks[t], 0:FC], ACT.Silu,
                                   scale=rstd[:, t:t + 1]).then_inc(silu_done, 1)

            def chunk(c, last=False):
                convert_act(act, ffn_piece(s, "C", c - 1), n0 + 1, c)
                split_act(act, s.fill0 + c - 1, psum[:, 6, :], hidT_views(hidT_hi))
                if last:
                    converts(act, convert_act, n0 + 3 * CHUNKS - 1)
                else:
                    convert_act(act, ffn_piece(s, "A", c + 1), n0 + 2, c)
                gate(c, UP[1])
                if last:
                    converts(act, convert_act, n0 + 3 * CHUNKS)
                else:
                    convert_act(act, ffn_piece(s, "B", c + 1), n0 + 3, c)

            converts(act, convert_act, n0 + 2, n0 + 3)
            act.wait_ge(rstd_done, 2 * (s.index + 1))
            gate(0, UP[0])
            chunk(1)
            with act.Fori(2, CHUNKS - 1) as c:
                chunk(c)
            chunk(CHUNKS - 1, last=True)
            split_act(act, s.fill0 + CHUNKS - 1, psum[:, 6, :], hidT_views(hidT_hi))
            converts(act, convert_act, n0 + 3 * CHUNKS + 1)

        def ffn_dve(dve, s):
            n0, b0 = s.piece0, s.block0

            def product(c, banks):
                for t in range(TT):
                    dve.wait_ge(silu_done, 2 * CHUNKS * s.ffn + t + 1 + 2 * c)
                    dve.scalar_tensor_tensor(hid[:, t, :], psum[:, banks[t], FC:2 * FC], rstd[:, t:t + 1],
                                             silu[:, t, :], op0=ALU.mult, op1=ALU.mult).then_inc(proj_read, 1)

            def split(c):
                split_dve(dve, s.fill0 + c, psum[:, 6, :], hidT_views(hidT_hi), hidT_views(hidT_lo))

            def chunk(c, last=False):
                convert_dve(dve, ffn_piece(s, "C", c - 1), n0 + 1, c)
                split(c - 1)
                if last:
                    converts(dve, convert_dve, n0 + 3 * CHUNKS - 1)
                else:
                    convert_dve(dve, ffn_piece(s, "A", c + 1), n0 + 2, c)
                product(c, UP[1])
                if last:
                    converts(dve, convert_dve, n0 + 3 * CHUNKS)
                else:
                    convert_dve(dve, ffn_piece(s, "B", c + 1), n0 + 3, c)

            converts(dve, convert_dve, n0 + 2, n0 + 3)
            dve.wait_ge(rstd_done, 2 * (s.index + 1))
            product(0, UP[0])
            chunk(1)
            with dve.Fori(2, CHUNKS - 1) as c:
                chunk(c)
            chunk(CHUNKS - 1, last=True)
            split(CHUNKS - 1)
            converts(dve, convert_dve, n0 + 3 * CHUNKS + 1)

        def block_wait(eng, s, b, t, last):
            if t == 0:
                eng.wait_ge(proj_done, s.block0 + b + 1)
            else:
                eng.wait_ge(piece_used, s.piece0 + last + 1)

        def block_piece(pe, s, b, n, k0, first, last):
            m = s.piece0 + n
            p = piece_at(m)
            pe.wait_ge(lo_ready, m + 1)
            for t in range(TT):
                i = project(pe, m % RING, t, UP[b % 2][t], k0, p.tiles, p.cols, first, last)
                if last and t == 0:
                    i.then_inc(proj_done, 1)
            i.then_inc(piece_used, 1)

        def plain_fill(pe, s, f, bank, blocks_in, width):
            if f >= 2:
                pe.wait_ge(plain_read, s.plain0 + f - 1)
            for j, b in enumerate(blocks_in):
                i = pe.transpose(psum[0:width, bank, j * P:(j + 1) * P], b, ident[:, :])
            i.then_inc(plain_T, 1)

        def y_fill_q(s):
            return s.norm_fill0 - 4

        def out_pe(pe, s):
            for f, (nh, t) in enumerate(GROUPS):
                pe.wait_ge(y_ready, s.y0 + (f + 1 if s.kind == "ml" else 2 * nh + 2))
                if f >= 2:
                    pe.wait_ge(tr_read, y_fill_q(s) + f - 1)
                fill_pe(pe, y, 4 + f % 2, t, nh)
            for a in range(3):
                pe.wait_ge(lo_ready, s.out0 + a + 1)
                pe.wait_ge(tr_read, y_fill_q(s) + (2 if a < 2 else 4))
                for g in range(4):
                    i = out_group(pe, (s.out0 + a) % RING, g, xT_hi, xT_lo, 2 * a, a == 0, False)
                i.then_inc(piece_used, 1)
            last_piece(pe, s, s.out0 + 3, xT_hi, xT_lo, 6)

        def y_splits(eng, s):
            for f, (nh, t) in enumerate(GROUPS):
                fill_split(eng, y_fill_q(s) + f, 4 + f % 2, t, 4 * nh)

        def evacuate(dve, s, b, last, dst, scale=None):
            for t in range(TT):
                block_wait(dve, s, b, t, last)
                src = psum[:, UP[b % 2][t], 0:dst.shape[2]]
                if scale is None:
                    i = dve.tensor_scalar(dst[:, t, :], src, rstd[:, t:t + 1], None, ALU.mult)
                else:
                    i = dve.tensor_scalar(dst[:, t, :], src, rstd[:, t:t + 1], scale, ALU.mult, ALU.mult)
                i.then_inc(proj_read, 1)

        def scores_pe(pe, g, bank, k_even, k_odd, q, start):
            for hh in range(GROUP):
                pair, k = 2 * g + hh // 2, (k_even, k_odd)[hh % 2]
                pe.matmul(psum[:, bank + hh // 2, hh % 2 * SEQ:(hh % 2 + 1) * SEQ], k[:, pair, 0:P], q[:, pair, :],
                          start=start and hh % 2 == 0, stop=hh % 2 == 1, skip_group_check=True)
            for hh in range(GROUP):
                pair, k = 2 * g + hh // 2, (k_even, k_odd)[hh % 2]
                i = pe.matmul(psum[:, bank + 2, hh * P:(hh + 1) * P], k[:, pair, P:SEQ], q[:, pair, P:SEQ],
                              start=start and hh == 0, stop=hh == 3, skip_group_check=True)
            return i

        def mask_pe(pe, m, bank):
            for b in range(3):
                pe.matmul(psum[:, bank + b, :], ident_b[:, :], mask[:, 2 * m + b // 2, :], start=True, stop=False,
                          skip_group_check=True)

        def banks3(bank):
            return psum[:, bank:bank + 3, :].rearrange("p b n -> p (b n)")

        def magnitude(dve, dst, src):
            return dve.tensor_scalar(dst.bitcast(I32), src.bitcast(I32), 0x7FFFFFFF, None, ALU.bitwise_and)

        def sb_pe(pe, s):
            pe.wait_ge(tr_read, norm_fill0(s.index) + 4)
            for b in range(6):
                if b:
                    if b >= 2:
                        pe.wait_ge(proj_read, 2 * (s.block0 + b - 1))
                    block_piece(pe, s, b, 2 * b, 0, True, False)
                if 1 <= b <= 4:
                    pe.wait_ge(proj_read, 2 * (s.block0 + b))
                    for t in range(TT):
                        plain_fill(pe, s, 2 * (b - 1) + t, 6 + t,
                                   [stage[:, t, j * P:(j + 1) * P] for j in range(4)], P)
                block_piece(pe, s, b, 2 * b + 1, 4, False, True)

            def scores(g):
                if g >= 2:
                    pe.wait_ge(w_done, 4 * s.inst + g - 1)
                mask_pe(pe, 0, 3 * (g % 2))
                scores_pe(pe, g, 3 * (g % 2), kT_even, kT_odd, qT, False).then_inc(z_done, 1)

            def remainder(g):
                bank, sp3 = 3 * (g % 2), sb_sp[:, g % 2, :]
                pe.wait_ge(sp_done, 4 * s.inst + g + 1)
                for b in range(3):
                    pe.matmul(psum[:, bank + b, :], neg_tri[:, :], sp3[:, b * NCOL:(b + 1) * NCOL], start=False,
                              stop=b == 2, skip_group_check=True)
                for b in range(2):
                    i = pe.matmul(psum[:, bank + b, :].rearrange("p (a n) -> p a n", a=2)[:, :, P:SEQ], neg_ones[:, :],
                                  sp3[:, 2 * NCOL + b * SEQ:2 * NCOL + (b + 1) * SEQ].rearrange("p (a n) -> p a n", a=2),
                                  start=False, stop=True, skip_group_check=True)
                i.then_inc(r_done, 1)

            def values(g):
                w3 = sb_e[:, g % 2, :]
                pe.wait_ge(w_done, 4 * s.inst + g + 1)
                if g >= 2:
                    pe.wait_ge(y_ready, s.y0 + g - 1)
                for t in range(TT):
                    for hh in range(GROUP):
                        c = (GROUP * g + hh) * 64
                        dst = psum[:, 6 + g % 2, (t * GROUP + hh) * 64:(t * GROUP + hh + 1) * 64]
                        i = pe.matmul(dst, w3[:, hh * SEQ + t * P:hh * SEQ + (t + 1) * P], v_sb[:, 0, c:c + 64],
                                      start=t == 0 and hh == 0, stop=t == 0, skip_group_check=True)
                        if t:
                            i = pe.matmul(dst, w3[:, 2 * NCOL + hh * P:2 * NCOL + (hh + 1) * P], v_sb[:, 1, c:c + 64],
                                          start=False, stop=True, skip_group_check=True)
                i.then_inc(av_done, 1)

            pe.wait_ge(pad_ready, s.pads)
            pe.wait_ge(plain_read, s.plain0 + 8)
            pe.wait_ge(proj_read, 2 * (s.block0 + 6))
            scores(0)
            for g in range(4):
                if g < 3:
                    scores(g + 1)
                if g:
                    values(g - 1)
                remainder(g)
            values(3)

        def sb_act(act, s, link):
            act.wait_ge(pad_ready, s.pads)
            for b in range(6):
                converts(act, convert_act, s.piece0 + 2 * b + 2)
                if 1 <= b <= 4:
                    for t in range(TT):
                        f = 2 * (b - 1) + t
                        act.wait_ge(plain_T, s.plain0 + f + 1)
                        bank = psum[:, 6 + t, :].rearrange("p (j n) -> p j n", j=4)
                        pairs, cols = slice(4 * ((b - 1) % 2), 4 * ((b - 1) % 2) + 4), slice(t * P, (t + 1) * P)
                        if b <= 2:
                            act.activation(kT_even[0:64, pairs, cols], bank[0:64, :, :], ACT.Copy)
                            act.activation(kT_odd[64:P, pairs, cols], bank[64:P, :, :], ACT.Copy).then_inc(plain_read, 1)
                        else:
                            act.activation(qT[:, pairs, cols], bank, ACT.Copy).then_inc(plain_read, 1)
                converts(act, convert_act, s.piece0 + 2 * b + 3)

            def log1p(g):
                e = sb_e[:, g % 2, :]
                act.wait_ge(abs_done, 4 * s.inst + g + 1)
                act.activation(e, e, ACT.Exp, scale=-1.0).then_inc(exp_done, 1)
                act.wait_ge(exp_done, 4 * s.inst + g + 1)
                act.activation(e, e, ACT.Ln, bias=1.0).then_inc(ln_done, 1)

            def weights(g):
                act.wait_ge(r_done, 4 * s.inst + g + 1)
                act.activation(sb_e[:, g % 2, :], banks3(3 * (g % 2)), ACT.Exp).then_inc(w_done, 1)

            log1p(0)
            for g in range(4):
                if g < 3:
                    log1p(g + 1)
                weights(g)
            y_splits(act, s)

        def sb_dve(dve, s, link):
            for b in range(6):
                converts(dve, convert_dve, s.piece0 + 2 * b + 2)
                if b == 1:
                    dve.wait_ge(rstd_done, 2 * (s.index + 1))
                if b:
                    dst = stage if b <= 4 else v_sb[:, :, 0:NCOL]
                    evacuate(dve, s, b - 1, 2 * b - 1, dst, SB_SCALE if b in (3, 4) else None)
                converts(dve, convert_dve, s.piece0 + 2 * b + 3)
            evacuate(dve, s, 5, 11, v_sb[:, :, NCOL:D])

            def absolute(g):
                dve.wait_ge(z_done, 4 * s.inst + g + 1)
                if g >= 2:
                    dve.wait_ge(av_done, 4 * s.inst + g - 1)
                magnitude(dve, sb_e[:, g % 2, :], banks3(3 * (g % 2))).then_inc(abs_done, 1)

            def softplus(g):
                dve.wait_ge(ln_done, 4 * s.inst + g + 1)
                dve.scalar_tensor_tensor(sb_sp[:, g % 2, :], banks3(3 * (g % 2)), 0.0, sb_e[:, g % 2, :],
                                         op0=ALU.max, op1=ALU.add).then_inc(sp_done, 1)

            def heads(g):
                dve.wait_ge(av_done, 4 * s.inst + g + 1)
                dve.tensor_copy(y[:, :, g * SEQ:(g + 1) * SEQ],
                                psum[:, 6 + g % 2, :].rearrange("p (t n) -> p t n", t=TT)).then_inc(y_ready, 1)

            absolute(0)
            for g in range(4):
                if g < 3:
                    absolute(g + 1)
                softplus(g)
                if g:
                    heads(g - 1)
            heads(3)
            y_splits(dve, s)

        def sb_pool(pool, s, link):
            pool.memset(kT_even, 0.0)
            pool.memset(kT_odd, 0.0).then_inc(pad_ready, 1)

        def ml_pe(pe, s):
            pe.wait_ge(tr_read, norm_fill0(s.index) + 4)
            for b in range(1, 7):
                if b >= 2:
                    pe.wait_ge(proj_read, 2 * (s.block0 + b - 1))
                block_piece(pe, s, b, 2 * b - 1, 0, True, False)
                if b == 1:
                    pe.wait_ge(proj_read, 2 * (s.block0 + 1))
                    for c in range(2):
                        for t in range(TT):
                            i = pe.transpose(psum[0:ML_HEADS, 6, (c * TT + t) * P:(c * TT + t + 1) * P],
                                             gate_in[:, t, c * ML_HEADS:(c + 1) * ML_HEADS], ident[:, :])
                    i.then_inc(gate_T_done, 1)
                if b in (2, 3):
                    pe.wait_ge(proj_read, 2 * (s.block0 + b))
                    if b == 2:
                        pe.wait_ge(gate_abs, 1)
                    for t in range(TT):
                        plain_fill(pe, s, 2 * (b - 2) + t, 6 + t, [stage[:, t, j * P:(j + 1) * P] for j in range(4)], P)
                if b == 4:
                    pe.wait_ge(gate_em, 1)
                    pe.wait_ge(plain_read, s.plain0 + 4)
                    for c, rows in enumerate((g_a, g_em)):
                        for t in range(TT):
                            i = pe.transpose(psum[:, 6, (c * TT + t) * ML_HEADS:(c * TT + t + 1) * ML_HEADS],
                                             rows[:, t * P:(t + 1) * P], ident[0:ML_HEADS, 0:ML_HEADS])
                    i.then_inc(gate_back, 1)
                block_piece(pe, s, b, 2 * b, 4, False, True)

            def numerators(g):
                pe.wait_ge(sw_done, g + 1)
                for t in range(TT):
                    for hh in range(GROUP):
                        c = (GROUP * g + hh) * P
                        parts = [(ml_sw[:, hh * SEQ + t * P:hh * SEQ + (t + 1) * P], 0)]
                        if t:
                            parts.append((ml_sw[:, 2 * NCOL + hh * P:2 * NCOL + (hh + 1) * P], 1))
                        for n, (w, kt) in enumerate(parts):
                            pe.matmul(psum[:, 6 + t, hh * P:(hh + 1) * P], w, mv[:, kt, c:c + P],
                                      start=hh == 0 and n == 0, stop=n == t, skip_group_check=True)
                        for n, (w, kt) in enumerate(parts):
                            i = pe.matmul(psum[:, 3, t * GROUP + hh:t * GROUP + hh + 1], w, ones[:, 0:1],
                                          start=t == 0 and hh == 0 and n == 0, stop=n == t, skip_group_check=True)
                i.then_inc(num_done, 1)

            pe.wait_ge(mqk_ready, 2)
            pe.wait_ge(proj_read, 2 * (s.block0 + 7))
            pe.wait_ge(gate_cols, 1)
            for g in range(2):
                if g:
                    pe.wait_ge(num_read, 1)
                scores_pe(pe, g, 0, mkT_even, mkT_odd, mqT, True).then_inc(s_done, 1)
                mask_pe(pe, 1, 3)
                for hh in range(GROUP):
                    pe.matmul(psum[:, 3 + hh // 2, hh % 2 * SEQ:(hh % 2 + 1) * SEQ], sel[:, GROUP * g + hh, :], g_M,
                              start=False, stop=hh % 2 == 1, skip_group_check=True)
                for hh in range(GROUP):
                    i = pe.matmul(psum[:, 5, hh * P:(hh + 1) * P], sel[:, GROUP * g + hh, :], g_M[:, P:SEQ],
                                  start=False, stop=hh == 3, skip_group_check=True)
                i.then_inc(lw_done, 1)
                numerators(g)

        def ml_act(act, s, link):
            act.wait_ge(pad_ready, s.pads)
            converts(act, convert_act, s.piece0 + 2)
            for b in range(1, 7):
                converts(act, convert_act, s.piece0 + 2 * b + 1)
                if b in (2, 3):
                    for t in range(TT):
                        act.wait_ge(plain_T, s.plain0 + 2 * (b - 2) + t + 1)
                        act.activation(conv_in[:, 4 * (b - 2):4 * (b - 1), 3 + t * P:3 + (t + 1) * P],
                                       psum[:, 6 + t, :].rearrange("p (j n) -> p j n", j=4),
                                       ACT.Copy).then_inc(plain_read, 1)
                if b == 2:
                    act.wait_ge(gate_abs, 1)
                    link(act.activation(g_t, g_t, ACT.Exp, scale=-1.0))
                    act.activation(g_t, g_t, ACT.Ln, bias=1.0).then_inc(gate_ln, 1)
                if b == 3:
                    act.wait_ge(gate_m, 1)
                    act.activation(g_em, g_t, ACT.Exp, scale=-1.0).then_inc(gate_em, 1)
                if b == 4:
                    act.wait_ge(conv_done, 1)
                    act.activation(mqT, conv_out[:, 0:4, :], ACT.Silu).then_inc(mqk_ready, 1)
                if b == 5:
                    act.wait_ge(conv_done, 2)
                    act.activation(mkT_even[0:64, :, :], conv_out[0:64, 4:8, :], ACT.Silu)
                    act.activation(mkT_odd[64:P, :, :], conv_out[64:P, 4:8, :], ACT.Silu).then_inc(mqk_ready, 1)
                converts(act, convert_act, s.piece0 + 2 * b + 2)
            for half in range(2):
                act.wait_ge(proj_read, 2 * (s.block0 + 6 + half))
                act.activation(mo[:, :, half * NCOL:(half + 1) * NCOL], mo[:, :, half * NCOL:(half + 1) * NCOL],
                               ACT.Sigmoid).then_inc(mo_ready, 1)
            act.wait_ge(gate_cols, 1)
            for g in range(2):
                act.wait_ge(lw_done, g + 1)
                if g:
                    act.wait_ge(sw_done, 1)
                for hh in range(GROUP):
                    head, c = GROUP * g + hh, hh * SEQ
                    act.activation(ml_wt[:, c:c + SEQ], psum[:, 3 + hh // 2, hh % 2 * SEQ:(hh % 2 + 1) * SEQ], ACT.Exp,
                                   bias=gate_T[:, 0, head:head + 1])
                for hh in range(GROUP):
                    head, c = GROUP * g + hh, 2 * NCOL + hh * P
                    i = act.activation(ml_wt[:, c:c + P], psum[:, 5, hh * P:(hh + 1) * P], ACT.Exp,
                                       bias=gate_T[:, 1, head:head + 1])
                i.then_inc(wt_done, 1)
            act.wait_ge(num_read, 2)
            for t in range(TT):
                act.activation(ml_sq[:, t, :], y[:, t, :], ACT.Square).then_inc(msq_done, 1)
            y_splits(act, s)

        def ml_dve(dve, s, link):
            dve.wait_ge(rstd_done, 2 * (s.index + 1))
            dve.wait_ge(pad_ready, s.pads)
            converts(dve, convert_dve, s.piece0 + 2)
            evacuate(dve, s, 0, 0, gate_in)
            for b in range(1, 7):
                converts(dve, convert_dve, s.piece0 + 2 * b + 1)
                if b >= 2:
                    dst = {2: stage, 3: stage, 4: mv[:, :, 0:NCOL], 5: mv[:, :, NCOL:D], 6: mo[:, :, 0:NCOL]}[b]
                    evacuate(dve, s, b - 1, 2 * b - 2, dst)
                if b == 1:
                    dve.wait_ge(gate_T_done, 1)
                    dve.tensor_scalar(g_i, psum[0:ML_HEADS, 6, 0:SEQ], gate_bias[:, 0:1], None, ALU.add)
                    link(dve.tensor_scalar(g_f, psum[0:ML_HEADS, 6, SEQ:2 * SEQ], gate_bias[:, 1:2], None, ALU.add))
                    dve.tensor_scalar(g_min, g_f, 0.0, None, ALU.min)
                    magnitude(dve, g_t, g_f).then_inc(gate_abs, 1)
                if b == 3:
                    dve.wait_ge(gate_ln, 1)
                    link(dve.tensor_tensor(g_f, g_min, g_t, ALU.subtract))
                    link(dve.tensor_tensor_scan(g_F, g_one, g_f, 0.0, ALU.mult, ALU.add))
                    link(dve.tensor_tensor(g_a, g_i, g_F, ALU.subtract))
                    link(dve.tensor_tensor_scan(g_M[0:ML_HEADS, :], g_a, g_a, 0.0, ALU.max, ALU.max))
                    dve.tensor_tensor(g_t, g_F, g_M[0:ML_HEADS, :], ALU.add).then_inc(gate_m, 1)
                if b in (3, 4):
                    part = b - 3
                    dve.wait_ge(plain_read, s.plain0 + 2 * (part + 1))
                    for j in (3, 2, 1, 0):
                        for k in range(4 * part, 4 * part + 4):
                            w = gains2[:, CONV_W + j * KD + k:CONV_W + j * KD + k + 1]
                            if j == 3:
                                i = dve.tensor_scalar(conv_out[:, k, :], conv_in[:, k, 3:3 + SEQ], w, None, ALU.mult)
                            else:
                                i = dve.scalar_tensor_tensor(conv_out[:, k, :], conv_in[:, k, j:j + SEQ], w,
                                                             conv_out[:, k, :], op0=ALU.mult, op1=ALU.add)
                        if j:
                            link(i)
                    i.then_inc(conv_done, 1)
                if b == 5:
                    dve.wait_ge(gate_back, 1)
                    dve.tensor_copy(gate_T, psum[:, 6, 0:4 * ML_HEADS].rearrange("p (c h) -> p c h", c=4)).then_inc(gate_cols, 1)
                converts(dve, convert_dve, s.piece0 + 2 * b + 2)
            evacuate(dve, s, 6, 12, mo[:, :, NCOL:D])
            dve.wait_ge(gate_cols, 1)
            for g in range(2):
                dve.wait_ge(s_done, g + 1)
                dve.wait_ge(wt_done, g + 1)
                dve.scalar_tensor_tensor(ml_sw, banks3(0), ML_SCALE, ml_wt, op0=ALU.mult,
                                         op1=ALU.mult).then_inc(sw_done, 1)
                dve.wait_ge(num_done, g + 1)
                link(magnitude(dve, den, psum[:, 3, 0:TT * GROUP].rearrange("p (t h) -> p t h", t=TT)))
                link(dve.tensor_tensor(den, den, gate_T[:, 2:4, GROUP * g:GROUP * (g + 1)], ALU.max))
                link(dve.reciprocal(den, den))
                for t in range(TT):
                    i = dve.tensor_tensor(y[:, t, g * NCOL:(g + 1) * NCOL].rearrange("p (h v) -> p h v", h=GROUP),
                                          psum[:, 6 + t, :].rearrange("p (h v) -> p h v", h=GROUP),
                                          den[:, t, :].unsqueeze(2).broadcast_to((P, GROUP, P)), ALU.mult)
                i.then_inc(num_read, 1)
            for t in range(TT):
                dve.wait_ge(msq_done, t + 1)
                dve.tensor_reduce(mssq[:, t, :], ml_sq[:, t, :].rearrange("p (h v) -> p h v", h=ML_HEADS), AX,
                                  ALU.add).then_inc(mssq_done, 1)
            dve.wait_ge(mo_ready, 2)
            dve.wait_ge(mrms_done, 1)
            for nh, t in GROUPS:
                ys, c = y[:, t, nh * NCOL:(nh + 1) * NCOL], slice(nh * NCOL, (nh + 1) * NCOL)
                link(dve.tensor_tensor(ys.rearrange("p (h v) -> p h v", h=GROUP), ys.rearrange("p (h v) -> p h v", h=GROUP),
                                       mrms[:, t, GROUP * nh:GROUP * (nh + 1)].unsqueeze(2).broadcast_to((P, GROUP, P)),
                                       ALU.mult))
                dve.tensor_tensor(ys, ys, mo[:, t, c], ALU.mult).then_inc(y_ready, 1)
            y_splits(dve, s)

        def ml_pool(pool, s, link):
            pool.memset(conv_in[:, :, 0:3], 0.0)
            pool.memset(mkT_even, 0.0)
            pool.memset(mkT_odd, 0.0)
            pool.memset(g_M, 0.0)
            pool.memset(g_one, 1.0)
            link(pool.memset(sel, 0.0))
            pool.affine_select(out=sel, in_=sel, compare_op=ALU.not_equal, fill=-1.0, base=0,
                               pattern=[[-1, ML_HEADS], [0, P]], channel_multiplier=1).then_inc(pad_ready, 1)
            pool.wait_ge(mssq_done, 2)
            link(pool.tensor_scalar(mssq, mssq, 1.0 / P, EPS, ALU.mult, ALU.add))
            pool.tensor_tensor(mrms.rearrange("p t h -> p (t h)"), mssq.rearrange("p t h -> p (t h)"), minus_half[:, :],
                               ALU.pow).then_inc(mrms_done, 1)

        def latent_fill_args(f):
            return 6 + f % 2, ([(f, k) for k in range(4)] if f < 2 else [(0, 4), (1, 4)])

        def latent_split(eng, s, f):
            bank, parts = latent_fill_args(f)
            if f < 2:
                fill_split(eng, s.fill0 + f, bank, f, 0)
            elif eng is nc.scalar:
                split_act(eng, s.fill0 + f, psum[:, bank, 0:SEQ], xT_hi[:, 4, :])
            else:
                split_dve(eng, s.fill0 + f, psum[:, bank, 0:SEQ], xT_hi[:, 4, :], xT_lo[:, 4, :])

        def lt_pe(pe, s):
            pe.wait_ge(tr_read, norm_fill0(s.index) + 4)
            block_piece(pe, s, 0, 1, 4, False, True)
            block_piece(pe, s, 1, 2, 0, True, True)
            pe.wait_ge(proj_read, 2 * (s.block0 + 2))
            for f in range(3):
                bank, parts = latent_fill_args(f)
                if f == 2:
                    pe.wait_ge(tr_read, s.fill0 + 1)
                for j, (t, k) in enumerate(parts):
                    i = pe.transpose(psum[:, bank, j * P:(j + 1) * P], lc[:, t, k * P:(k + 1) * P], ident[:, :])
                i.then_inc(tr_done, 1)
            pe.wait_ge(tr_read, s.fill0 + 3)

            def heads_T(b):
                if b < 6:
                    pe.wait_ge(lstage_ready, b - 1)
                else:
                    pe.wait_ge(proj_read, 2 * (s.block0 + b + 1))
                src = lq if b < 6 else lk
                for t in range(TT):
                    plain_fill(pe, s, 2 * (b - 2) + t, 6 + t, [src[:, t * GROUP + hh, :] for hh in range(GROUP)], QK)

            for b in range(2, 10):
                pe.wait_ge(proj_read, 2 * (s.block0 + b - 1))
                block_piece(pe, s, b, b + 1, 0 if b < 6 else 3, True, True)
                if b > 2:
                    heads_T(b - 1)
            heads_T(9)

            def scores(g):
                if g:
                    pe.wait_ge(sub_done, g)
                mask_pe(pe, 2, 0)
                for hh in range(GROUP):
                    n = GROUP * g + hh
                    pe.matmul(psum[:, hh // 2, hh % 2 * SEQ:(hh % 2 + 1) * SEQ], lqT[0:QK, n, P:SEQ], lkT[0:QK, n, :],
                              start=False, stop=hh % 2 == 1, skip_group_check=True)
                for hh in range(GROUP):
                    n = GROUP * g + hh
                    i = pe.matmul(psum[:, 2, hh * P:(hh + 1) * P], lqT[0:QK, n, 0:P], lkT[0:QK, n, 0:P],
                                  start=False, stop=hh == 3, skip_group_check=True)
                i.then_inc(sc_done, 1)

            def transposes(g):
                pe.wait_ge(px_done, g + 1)
                if g:
                    pe.wait_ge(pT_read, g)
                for n, (start, step) in enumerate(((0, SEQ), (P, SEQ), (2 * NCOL, P))):
                    for hh in range(GROUP):
                        c = start + hh * step
                        i = pe.transpose(psum[:, 3 + n, hh * P:(hh + 1) * P], l_px[:, c:c + P], ident[:, :])
                i.then_inc(pT_done, 1)

            def values(g):
                pe.wait_ge(pT_read, g + 1)
                if g >= 2:
                    pe.wait_ge(y_ready, s.y0 + g - 1)
                for t in range(TT):
                    for hh in range(GROUP):
                        c = (GROUP * g + hh) * VD
                        dst = psum[:, 6 + g % 2, (t * GROUP + hh) * VD:(t * GROUP + hh + 1) * VD]
                        parts = [(2, 0)] if t == 0 else [(0, 0), (1, 1)]
                        for n, (part, kt) in enumerate(parts):
                            i = pe.matmul(dst, l_pT[:, part * NCOL + hh * P:part * NCOL + (hh + 1) * P],
                                          lv[:, kt, c:c + VD], start=t == 0 and hh == 0, stop=n == t,
                                          skip_group_check=True)
                i.then_inc(lav_done, 1)

            pe.wait_ge(plain_read, s.plain0 + 16)
            pe.wait_ge(proj_read, 2 * (s.block0 + 10))
            scores(0)
            for g in range(4):
                if g < 3:
                    scores(g + 1)
                transposes(g)
                if g:
                    values(g - 1)
            values(3)

        def lt_act(act, s, link):
            converts(act, convert_act, s.piece0 + 2, s.piece0 + 3)
            act.wait_ge(angle_done, 1)
            act.activation(trig, angle, ACT.Sin).then_inc(trig_done, 1)
            converts(act, convert_act, s.piece0 + 4)
            act.wait_ge(proj_read, 2 * (s.block0 + 2))
            for f in range(3):
                latent_split(act, s, f)
            for n, (a, b) in enumerate(((0, Q_RANK), (Q_RANK, Q_RANK + KV_RANK))):
                for t in range(TT):
                    scratch = l_pT[:, TT * a + t * (b - a):TT * a + (t + 1) * (b - a)]
                    i = act.activation(scratch, lc[:, t, a:b], ACT.Square, accum_out=lssq[:, n, t:t + 1])
            i.then_inc(lssq_done, 1)
            for b in range(2, 11):
                if b > 2:
                    dst = lqT if b - 1 < 6 else lkT
                    for t in range(TT):
                        act.wait_ge(plain_T, s.plain0 + 2 * (b - 3) + t + 1)
                        h0 = GROUP * ((b - 3) % 4)
                        act.activation(dst[0:QK, h0:h0 + GROUP, t * P:(t + 1) * P],
                                       psum[0:QK, 6 + t, :].rearrange("p (j n) -> p j n", j=4),
                                       ACT.Copy).then_inc(plain_read, 1)
                if b < 10:
                    converts(act, convert_act, s.piece0 + b + 3)

            def exps(g):
                act.wait_ge(sub_done, g + 1)
                act.activation(l_px, l_px, ACT.Exp).then_inc(px_done, 1)

            exps(0)
            for g in range(4):
                act.wait_ge(pT_done, g + 1)
                if g:
                    act.wait_ge(lav_done, g)
                act.activation(l_pT, banks3(3), ACT.Copy).then_inc(pT_read, 1)
                if g < 3:
                    exps(g + 1)
            y_splits(act, s)

        def lt_dve(dve, s, link):
            converts(dve, convert_dve, s.piece0 + 2, s.piece0 + 3)
            dve.wait_ge(pad_ready, s.pads)
            link(dve.tensor_copy(pos_f, pos_i[:, :]))
            for n in range(4):
                i = dve.tensor_scalar(angle[:, n, :], inv_freq, pos_f[:, n % TT:n % TT + 1], None, ALU.mult)
            link(i)
            for n in range(4):
                i = dve.tensor_scalar(turns[:, n, :], angle[:, n, :], 1.0 / TWO_PI, 0.25 * (n // TT), ALU.mult, ALU.add)
            link(i)
            link(dve.tensor_scalar(turns, turns, ROUND, None, ALU.add))
            link(dve.tensor_scalar(turns, turns, ROUND, None, ALU.subtract))
            for part in TWO_PI_PARTS:
                link(dve.scalar_tensor_tensor(angle, turns, -part, angle, op0=ALU.mult, op1=ALU.add))
            link(dve.tensor_scalar(angle[:, TT:4, :], angle[:, TT:4, :], TWO_PI / 4, None, ALU.add))
            dve.tensor_scalar(angle, angle, -SIN_MAX, SIN_MAX, ALU.max, ALU.min).then_inc(angle_done, 1)
            converts(dve, convert_dve, s.piece0 + 4)
            dve.wait_ge(rstd_done, 2 * (s.index + 1))
            evacuate(dve, s, 0, 1, lc[:, :, 0:NCOL])
            evacuate(dve, s, 1, 2, lc[:, :, NCOL:MLA_IN])
            dve.wait_ge(proj_read, 2 * (s.block0 + 2))
            for f in range(3):
                latent_split(dve, s, f)
            dve.wait_ge(trig_done, 1)

            def rope(x1, x2, o1, o2, tmp, sin, cos):
                dve.tensor_tensor(tmp[0], x1, cos, ALU.mult)
                dve.tensor_tensor(tmp[1], x2, sin, ALU.mult)
                dve.tensor_tensor(tmp[2], x1, sin, ALU.mult)
                link(dve.tensor_tensor(tmp[3], x2, cos, ALU.mult))
                dve.tensor_tensor(o1, tmp[0], tmp[1], ALU.subtract)
                return dve.tensor_tensor(o2, tmp[2], tmp[3], ALU.add)

            kr_in = lc[:, :, Q_RANK + KV_RANK:MLA_IN]
            sin, cos = trig[:, 0:TT, :], trig[:, TT:4, :]
            link(rope(kr_in[:, :, 0:HALF], kr_in[:, :, HALF:ROPE], kr[:, :, 0:HALF], kr[:, :, HALF:ROPE],
                      [rope_tmp[:, n, 0:TT, :] for n in range(4)], sin, cos))
            for t in range(TT):
                dve.tensor_copy(lk[:, t * GROUP:(t + 1) * GROUP, NOPE:QK],
                                kr[:, t, :].unsqueeze(1).broadcast_to((P, GROUP, ROPE)))
            dve.wait_ge(lrms_done, 1)
            for b in range(2, 11):
                if b > 2:
                    c = b - 1
                    if c > 2:
                        dve.wait_ge(plain_T, s.plain0 + 2 * (c - 2))
                    for t in range(TT):
                        block_wait(dve, s, c, t, c + 1)
                        bank, hs = psum[:, UP[c % 2][t], :], slice(t * GROUP, (t + 1) * GROUP)
                        if c < 6:
                            i = dve.tensor_scalar(lq[:, hs, :], bank[:, 0:GROUP * QK].rearrange("p (h d) -> p h d", h=GROUP),
                                                  lrms[:, 0, t:t + 1], MLA_SCALE, ALU.mult, ALU.mult)
                            i.then_inc(proj_read, 1)
                        else:
                            kv = bank.rearrange("p (h d) -> p h d", h=GROUP)
                            dve.tensor_scalar(lk[:, hs, 0:NOPE], kv[:, :, 0:NOPE], lrms[:, 1, t:t + 1], None, ALU.mult)
                            c0 = (c - 6) * GROUP * VD
                            i = dve.tensor_scalar(lv[:, t, c0:c0 + GROUP * VD].rearrange("p (h d) -> p h d", h=GROUP),
                                                  kv[:, :, NOPE:NOPE + VD], lrms[:, 1, t:t + 1], None, ALU.mult)
                            i.then_inc(proj_read, 1)
                    if c < 6:
                        dve.wait_ge(proj_read, 2 * (s.block0 + c + 1))
                        for t in range(TT):
                            q4 = lq[:, t * GROUP:(t + 1) * GROUP, :]
                            x1, x2 = q4[:, :, NOPE:NOPE + HALF], q4[:, :, NOPE + HALF:QK]
                            sn, cs = (v[:, t, :].unsqueeze(1).broadcast_to((P, GROUP, HALF)) for v in (sin, cos))
                            i = rope(x1, x2, x1, x2, [rope_tmp[:, n, t * GROUP:(t + 1) * GROUP, :] for n in range(4)], sn, cs)
                        i.then_inc(lstage_ready, 1)
                if b < 10:
                    converts(dve, convert_dve, s.piece0 + b + 3)

            def softmax_in(g):
                dve.wait_ge(sc_done, g + 1)
                tiles = ((psum[:, 0:2, :].rearrange("p b (h n) -> p (b h) n", h=2), slice(0, 4), l_px[:, 0:2 * NCOL], SEQ),
                         (psum[:, 2, :].rearrange("p (h n) -> p h n", h=4), slice(4, 8), l_px[:, 2 * NCOL:3 * NCOL], P))
                for src, m, dst, n in tiles:
                    i = dve.tensor_reduce(lmax[:, m], src, AX, ALU.max)
                link(i)
                if g:
                    dve.wait_ge(pT_done, g)
                for src, m, dst, n in tiles:
                    i = dve.tensor_tensor(dst.rearrange("p (h n) -> p h n", h=4), src,
                                          lmax[:, m].unsqueeze(2).broadcast_to((P, 4, n)), ALU.subtract)
                i.then_inc(sub_done, 1)

            def sums(g):
                dve.wait_ge(px_done, g + 1)
                if g:
                    dve.wait_ge(y_ready, s.y0 + g)
                dve.tensor_reduce(lsum[:, 0:4], l_px[:, 0:2 * NCOL].rearrange("p (h n) -> p h n", h=4), AX, ALU.add)
                link(dve.tensor_reduce(lsum[:, 4:8], l_px[:, 2 * NCOL:3 * NCOL].rearrange("p (h n) -> p h n", h=4), AX, ALU.add))
                link(dve.reciprocal(lsum, lsum))

            def heads(g):
                dve.wait_ge(lav_done, g + 1)
                for t in range(TT):
                    i = dve.tensor_tensor(y[:, t, g * SEQ:(g + 1) * SEQ].rearrange("p (h v) -> p h v", h=GROUP),
                                          psum[:, 6 + g % 2, t * SEQ:(t + 1) * SEQ].rearrange("p (h v) -> p h v", h=GROUP),
                                          lsum[:, 4 - 4 * t:8 - 4 * t].unsqueeze(2).broadcast_to((P, GROUP, VD)), ALU.mult)
                i.then_inc(y_ready, 1)

            softmax_in(0)
            for g in range(4):
                sums(g)
                if g < 3:
                    softmax_in(g + 1)
                heads(g)
            y_splits(dve, s)

        def lt_pool(pool, s, link):
            for j in range(HALF):
                i = pool.memset(inv_freq[:, j:j + 1], ROPE_THETA ** (-j / HALF))
            i.then_inc(pad_ready, 1)
            pool.wait_ge(lssq_done, 1)
            for n, rank in enumerate((Q_RANK, KV_RANK)):
                i = pool.tensor_scalar(lms[:, n, :], lssq[:, n, :], 1.0 / rank, EPS, ALU.mult, ALU.add)
            link(i)
            pool.tensor_tensor(lrms.rearrange("p n t -> p (n t)"), lms.rearrange("p n t -> p (n t)"), minus_half[:, 0:4],
                               ALU.pow).then_inc(lrms_done, 1)

        MIXERS = {"sb": {"pe": sb_pe, "act": sb_act, "dve": sb_dve, "pool": sb_pool},
                  "ml": {"pe": ml_pe, "act": ml_act, "dve": ml_dve, "pool": ml_pool},
                  "mla": {"pe": lt_pe, "act": lt_act, "dve": lt_dve, "pool": lt_pool}}

        block = ctx.enter_context(nc.Block())

        @block.sync
        def _(sp):
            for t in range(TT):
                sp.dma_start(h[:, t, :], x[0, t * P:(t + 1) * P, :]).then_inc(x_loaded, 16)
            for s in subs:
                end = s.piece0 + s.n_pieces
                if s.kind != "ffn":
                    for n in range(s.piece0, end):
                        load(sp, piece_at(n), n)
                    continue
                for n in range(s.piece0, s.piece0 + 5):
                    load(sp, piece_at(n), n)
                with sp.Fori(2, CHUNKS) as c:
                    for r, role in enumerate("ABC"):
                        load(sp, ffn_piece(s, role, c if r < 2 else c - 1), s.piece0 - 1 + r, c)
                load(sp, piece_at(end - 1), end - 1)
            sp.dma_start(gain_row, ln_final.rearrange("(a n) -> a n", a=1).broadcast_to((P, D))).then_inc(gainrow_loaded, 16)
            for t in range(TT):
                sp.wait_ge(final_done, t + 1)
                sp.dma_start(out[0, t * P:(t + 1) * P, :], y[:, t, :]).then_inc(out_stored, 16)
            sp.wait_ge(out_stored, 16 * TT)

        @block.gpsimd
        def _(pool):
            chain = [0]

            def link(ins):
                chain[0] += 1
                ins.then_inc(pool_chain, 1)
                pool.wait_ge(pool_chain, chain[0])

            link(pool.memset(ident[:, :], 0.0))
            link(pool.affine_select(out=ident[:, :], in_=ident[:, :], compare_op=ALU.not_equal, fill=1.0, base=0,
                                    pattern=[[-1, P]], channel_multiplier=1))
            pool.memset(minus_half[:, :], -0.5)
            pool.memset(ones[:, :], 1.0)
            pool.memset(neg_ones[:, :], -1.0)
            link(pool.memset(neg_tri[:, :], -1.0))
            link(pool.affine_select(out=neg_tri[:, :], in_=neg_tri[:, :], compare_op=ALU.is_ge, fill=0.0, base=0,
                                    pattern=[[-1, P]], channel_multiplier=1))
            link(pool.tensor_copy(ident_b[:, :], ident[:, :]))
            link(pool.memset(mask[:, :, :], 0.0))
            for m, (base, mult, step) in enumerate(((0, -1, 1), (1, -1, 1), (1, 1, -1))):
                blocks4 = mask[:, 2 * m + 1, :].rearrange("p (a n) -> p a n", a=4)
                blocks2 = mask[:, 2 * m, :].rearrange("p (a b n) -> p a b n", a=2, b=2)
                for view in ([blocks4, blocks2[:, :, 1 if m == 2 else 0, :]]):
                    last = pool.affine_select(out=view, in_=view, compare_op=ALU.is_gt, fill=NEG, base=base,
                                              pattern=[[0, view.shape[1]], [step, P]], channel_multiplier=mult)
            last.then_inc(const_done, 1)
            for j in range(len(subs) + 1):
                for t in range(TT):
                    pool.wait_ge(ssq_done, TT * j + t + 1)
                    link(pool.tensor_scalar(mean_sq[:, t:t + 1], ssq[:, t:t + 1], 1.0 / D, EPS, ALU.mult, ALU.add))
                    pool.tensor_tensor(rstd[:, t:t + 1], mean_sq[:, t:t + 1], minus_half[:, 0:1],
                                       ALU.pow).then_inc(rstd_done, 1)
                if j < len(subs) and subs[j].kind != "ffn":
                    MIXERS[subs[j].kind]["pool"](pool, subs[j], link)

        @block.scalar
        def _(act):
            chain = [0]

            def act_link(ins):
                chain[0] += 1
                ins.then_inc(act_chain, 1)
                act.wait_ge(act_chain, chain[0])

            for a, g in enumerate((ln_ffn1, ln_mix, ln_ffn2)):
                act.dma_start(stage[a * DEPTH * KD:(a + 1) * DEPTH * KD, 0, 0:P],
                              g.rearrange("l (k p) -> (l k) p", p=P)).then_inc(par_loaded, 16)
            for at, n, v in ((GAIN_Q, 3, mla_g_q), (GAIN_KV, 2, mla_g_kv)):
                act.dma_start(stage[at:at + n, 1, 0:P], v[0, :].rearrange("(k p) -> k p", p=P)).then_inc(par_loaded, 16)
            act.dma_start(stage[GAIN_HEAD:GAIN_HEAD + KD, 1, 0:P], ml_head_gain[0, :, :]).then_inc(par_loaded, 16)
            act.dma_start(stage[CONV_W:CONV_W + 4 * KD, 1, 0:P],
                          ml_conv_w[0, :, :].rearrange("j (k p) -> (j k) p", p=P)).then_inc(par_loaded, 16)
            for col, b in enumerate((ml_b_igate, ml_b_fgate)):
                act.dma_start(gate_bias[:, col:col + 1], b[0, :].rearrange("(h a) -> h a", a=1)).then_inc(par_loaded, 16)
            act.dma_start(pos_i[:, :], positions[0, :].rearrange("(t p) -> p t", p=P),
                          allow_slow_non_contiguous=True).then_inc(par_loaded, 16)
            act.wait_ge(x_loaded, 16 * TT)
            act.wait_ge(gains_ready, 1)
            converts(act, convert_act, 0)
            norm_act(act, 0)
            converts(act, convert_act, 1)
            for s in subs:
                if s.kind == "ffn":
                    ffn_act(act, s)
                else:
                    MIXERS[s.kind]["act"](act, s, act_link)
                    for a in range(4):
                        converts(act, convert_act, s.out0 + a + 2)
                if s.index + 1 < len(subs):
                    norm_act(act, s.index + 1)
            for t in range(TT):
                act.wait_ge(h_done, 4 * len(subs) - 2 + 2 * t)
                act.activation(y[:, t, :], h[:, t, :], ACT.Square, accum_out=ssq[:, t:t + 1]).then_inc(ssq_done, 1)

        @block.vector
        def _(dve):
            chain = [0]

            def link(ins):
                chain[0] += 1
                ins.then_inc(dve_chain, 1)
                dve.wait_ge(dve_chain, chain[0])

            dve.wait_ge(par_T, 1)
            dve.tensor_copy(gains1[:, :], psum[:, 0, 0:N_GAINS_1])
            dve.tensor_copy(gains2[:, :], psum[:, 1, 0:N_GAINS_2]).then_inc(gains_ready, 1)
            dve.wait_ge(gains_ready, 1)
            converts(dve, convert_dve, 0)
            norm_dve(dve, 0, None)
            converts(dve, convert_dve, 1)
            for s in subs:
                if s.kind == "ffn":
                    ffn_dve(dve, s)
                else:
                    MIXERS[s.kind]["dve"](dve, s, link)
                    for a in range(4):
                        converts(dve, convert_dve, s.out0 + a + 2)
                norm_dve(dve, s.index + 1, 0.5 if s.kind == "ffn" else 1.0)
            dve.wait_ge(gainrow_loaded, 16)
            for t in range(TT):
                dve.wait_ge(rstd_done, TT * len(subs) + t + 1)
                dve.scalar_tensor_tensor(y[:, t, :], h[:, t, :], rstd[:, t:t + 1], gain_row, op0=ALU.mult,
                                         op1=ALU.mult).then_inc(final_done, 1)

        @block.tensor
        def _(pe):
            pe.wait_ge(const_done, 1)
            pe.wait_ge(par_loaded, 16 * 10)
            pe.transpose(psum[:, 0, 0:N_GAINS_1], stage[0:N_GAINS_1, 0, 0:P], ident[0:N_GAINS_1, 0:N_GAINS_1])
            pe.transpose(psum[:, 1, 0:N_GAINS_2], stage[0:N_GAINS_2, 1, 0:P],
                         ident[0:N_GAINS_2, 0:N_GAINS_2]).then_inc(par_T, 1)
            pe.wait_ge(gains_ready, 1)
            norm_fill(pe, 0, 0)
            first_piece(pe, 0)
            for s in subs:
                if s.kind == "ffn":
                    ffn_pe(pe, s)
                else:
                    MIXERS[s.kind]["pe"](pe, s)
                    out_pe(pe, s)


NAMES = ["x", "positions", "ln_ffn1", "ffn1_wi", "ffn1_wo", "ln_mix", "ln_ffn2", "ffn2_wi", "ffn2_wo",
         "sb_w_in", "sb_w_out", "ml_w_in", "ml_conv_w", "ml_b_igate", "ml_b_fgate", "ml_head_gain", "ml_w_out",
         "mla_w_in", "mla_g_q", "mla_w_uq", "mla_g_kv", "mla_w_ukv", "mla_w_out", "ln_final"]


def kernel(**inputs):
    import numpy as np
    import concourse.bacc as bacc
    from concourse.bass_utils import run_bass_kernel_spmd

    nc = bacc.Bacc("TRN2", target_bir_lowering=False, num_devices=1)
    arrays, args = {}, []
    for name in NAMES:
        a = np.ascontiguousarray(inputs[name])
        arrays[f"in_{name}"] = a
        args.append(nc.dram_tensor(f"in_{name}", a.shape, mybir.dt.from_np(a.dtype), kind="ExternalInput").ap())
    args.append(nc.dram_tensor("out_0", (1, SEQ, D), F32, kind="ExternalOutput").ap())
    trunk(nc, *args)
    r = run_bass_kernel_spmd(nc, [arrays], core_ids=[0])
    return r.results[0]["out_0"]
```

```python
from contextlib import ExitStack

import concourse.bass as bass
from concourse import mybir

F32 = mybir.dt.float32
F32R = mybir.dt.float32r
BF16 = mybir.dt.bfloat16
I32 = mybir.dt.int32
ACT = mybir.ActivationFunctionType
ALU = mybir.AluOpType
AX = mybir.AxisListType.X

P = 128
SEQ = 256
TT = SEQ // P
D = 1024
KD = D // P
NCOL = 512
HALVES = D // NCOL
EPS = 1e-6
DEPTH = 4
D_FF = 2816
FC = 256
CHUNKS = D_FF // FC
RING = 3
PCOLS = 2048
MIX_COLS = 16704
NEG = -1e30

SB_HEADS = 16
SB_SCALE = 64 ** -0.5
ML_HEADS = 8
ML_SCALE = 64 ** -0.5
MLA_HEADS = 16
NOPE, ROPE, VD = 64, 32, 64
QK = NOPE + ROPE
HALF = ROPE // 2
Q_RANK, KV_RANK = 384, 256
MLA_IN = Q_RANK + KV_RANK + ROPE
MLA_SCALE = QK ** -0.5
ROPE_THETA = 10000.0
TWO_PI = 6.283185307179586
TWO_PI_PARTS = (6.28125, 0.0019350051879882812, 3.019916050561733e-07)
ROUND = 1.5 * 2.0 ** 23
SIN_MAX = 3.1415925
GROUP = 4
GROUPS = [(t, nh) for t in range(TT) for nh in range(HALVES)]
UP = ((0, 1), (4, 5))
OWN = 1000

GAIN_FFN1, GAIN_MIX, GAIN_FFN2 = 0, DEPTH * KD, 2 * DEPTH * KD
GAIN_Q, GAIN_KV, GAIN_HEAD, CONV_W = 0, 3, 5, 13
N_GAINS_1 = 3 * DEPTH * KD
N_GAINS_2 = CONV_W + 4 * KD


def halves(n):
    return (0, n // 2), (n // 2, n)


class Sub:
    pass


class Piece:

    def __init__(self, tiles, cols, gain, sources):
        self.tiles, self.cols, self.gain, self.sources = tiles, cols, gain, sources


def rows_piece(w, k0, tiles, c0, cols, gain):
    v = w.rearrange("(k p) n -> p k n", p=P)
    if tiles > 1:
        cut = [(a, b, 0, cols) for a, b in ((0, tiles // 2), (tiles // 2, tiles))]
    else:
        cut = [(0, 1, a, b) for a, b in halves(cols)]
    return Piece(tiles, cols, gain,
                 [(a, b, ca, cb, v[:, k0 + a:k0 + b, c0 + ca:c0 + cb]) for a, b, ca, cb in cut])


def up_piece(wi, c, part, gain):
    v = wi.rearrange("(k p) (s n) -> p k s n", p=P, s=2)
    return Piece(4, 2 * FC, gain,
                 [(0, 4, s * FC, (s + 1) * FC, v[:, 4 * part:4 * part + 4, s, bass.ds(c * FC, FC)])
                  for s in range(2)])


def down_piece(wo, c):
    return Piece(2, D, None,
                 [(j, j + 1, 0, D, wo[bass.ds(c * FC + j * P, P), :].rearrange("(k p) n -> p k n", k=1))
                  for j in range(2)])


def trunk(nc, x, positions, ln_ffn1, ffn1_wi, ffn1_wo, ln_mix, ln_ffn2, ffn2_wi, ffn2_wo,
          sb_w_in, sb_w_out, ml_w_in, ml_conv_w, ml_b_igate, ml_b_fgate, ml_head_gain, ml_w_out,
          mla_w_in, mla_g_q, mla_w_uq, mla_g_kv, mla_w_ukv, mla_w_out, ln_final, out):
    ctx = ExitStack()
    with ctx:
        def sb(name, shape, dt=F32):
            return ctx.enter_context(nc.sbuf_tensor(name, shape, dt))

        def sem(name):
            return ctx.enter_context(nc.semaphore(name))

        raw = sb("raw", [P, RING, PCOLS])
        whi = sb("whi", [P, RING, PCOLS], F32R)
        wlo = sb("wlo", [P, RING, PCOLS], F32R)
        h = sb("h", [P, TT, D])
        xT_hi = sb("xT_hi", [P, KD, SEQ], F32R)
        xT_lo = sb("xT_lo", [P, KD, SEQ], F32R)
        hid = sb("hid", [P, TT, FC])
        silu = sb("silu", [P, TT, FC])
        hidT_hi = sb("hidT_hi", [P, FC // P, SEQ], F32R)
        hidT_lo = sb("hidT_lo", [P, FC // P, SEQ], F32R)
        y = sb("y", [P, TT, D])
        gains1 = sb("gains1", [P, N_GAINS_1])
        gains2 = sb("gains2", [P, N_GAINS_2])
        ident = sb("ident", [P, P])
        ident_b = sb("ident_b", [P, P], BF16)
        neg_tri = sb("neg_tri", [P, P])
        neg_ones = sb("neg_ones", [P, P])
        ones = sb("ones", [P, 2])
        mask = sb("mask", [P, 6, NCOL], BF16)
        ssq = sb("ssq", [P, TT])
        mean_sq = sb("mean_sq", [P, TT])
        rstd = sb("rstd", [P, TT])
        minus_half = sb("minus_half", [P, 16])
        gate_bias = sb("gate_bias", [ML_HEADS, 2])
        pos_i = sb("pos_i", [P, TT], I32)
        mix = sb("mix", [P, MIX_COLS])
        psum = ctx.enter_context(nc.psum_tensor("psum", [P, 8, NCOL], F32))

        def carve(start, *dims):
            n = 1
            for d in dims:
                n *= d
            assert start + n <= MIX_COLS, (start, n)
            v = mix[:, start:start + n]
            if len(dims) == 2:
                v = v.rearrange("p (a b) -> p a b", a=dims[0])
            if len(dims) == 3:
                v = v.rearrange("p (a b c) -> p a b c", a=dims[0], b=dims[1])
            return v, start + n

        stage, at0 = carve(0, TT, NCOL)
        qT, at = carve(at0, KD, SEQ)
        kT_even, at = carve(at, KD, SEQ)
        kT_odd, at = carve(at, KD, SEQ)
        v_sb, at = carve(at, TT, D)
        sb_e, at = carve(at, 2, 3 * NCOL)
        sb_sp, at = carve(at, 2, 3 * NCOL)
        mqT, at = carve(at0, 4, SEQ)
        mkT_even, at = carve(at, 4, SEQ)
        mkT_odd, at = carve(at, 4, SEQ)
        mv, at = carve(at, TT, D)
        mo, at = carve(at, TT, D)
        g_rows, at = carve(at, 9, SEQ)
        g_i, g_f, g_t, g_F, g_a, g_em, g_one, g_min = (g_rows[0:ML_HEADS, j, :] for j in range(8))
        g_M = g_rows[:, 8, :]
        gate_raw, at = carve(at, SEQ)
        gate_in, at = carve(at, TT, 2 * ML_HEADS)
        gate_T, at = carve(at, 4, ML_HEADS)
        den, at = carve(at, TT, GROUP)
        mssq, at = carve(at, 2, TT * GROUP)
        mrms, at = carve(at, 2, TT * GROUP)
        sel, at = carve(at, ML_HEADS, P)
        ml_wt = mix[:, at:at + 3 * NCOL]
        q_in, at = carve(at, 4, 3 + SEQ)
        q_out, at = carve(at, 4, SEQ)
        ml_sw = mix[:, at:at + 3 * NCOL]
        k_in, at = carve(at, 4, 3 + SEQ)
        k_out, at = carve(at, 4, SEQ)
        conv_in, conv_out = (q_in, k_in), (q_out, k_out)
        lqT, at = carve(0, MLA_HEADS, SEQ)
        lkT, at = carve(at, MLA_HEADS, SEQ)
        lv, at = carve(at, TT, D)
        lq, at = carve(at, TT * GROUP, QK)
        lk, at = carve(at, TT * GROUP, QK)
        angle, at = carve(at, 4, HALF)
        turns, at = carve(at, 4, HALF)
        trig, at = carve(at, 4, HALF)
        inv_freq, at = carve(at, HALF)
        kr, at = carve(at, TT, ROPE)
        rope_tmp, at = carve(at, 4, TT * GROUP, HALF)
        pos_f, at = carve(at, TT)
        lssq, at = carve(at, 2, TT)
        lms, at = carve(at, 2, TT)
        lrms, at = carve(at, 2, TT)
        lmax, at = carve(at, 8)
        lneg, at = carve(at, 8)
        lsum, at = carve(at, 2, 8)
        linv, at = carve(at, 8)
        lc, _ = carve(at, TT, MLA_IN)
        l_px, at = carve(at, 3 * NCOL)
        l_pT, at = carve(at, 3 * NCOL)
        gain_row, _ = carve(0, D)

        raw_loaded = [sem(f"raw_loaded{j}") for j in range(RING)]
        hi_ready = sem("hi_ready")
        lo_ready = sem("lo_ready")
        piece_used = sem("piece_used")
        proj_done = sem("proj_done")
        proj_read = sem("proj_read")
        silu_done = sem("silu_done")
        tr_done = sem("tr_done")
        tr_hi = sem("tr_hi")
        tr_read = sem("tr_read")
        acc_done = sem("acc_done")
        h_done = sem("h_done")
        ssq_done = sem("ssq_done")
        rstd_done = sem("rstd_done")
        x_loaded = sem("x_loaded")
        gains_loaded = sem("gains_loaded")
        par_loaded = sem("par_loaded")
        const_done = sem("const_done")
        par_T = sem("par_T")
        gains_ready = sem("gains_ready")
        y_ready = sem("y_ready")
        plain_T = sem("plain_T")
        plain_read = sem("plain_read")
        pad_ready = sem("pad_ready")
        z_done = sem("z_done")
        abs_done = sem("abs_done")
        exp_done = sem("exp_done")
        ln_done = sem("ln_done")
        sp_done = sem("sp_done")
        r_done = sem("r_done")
        w_done = sem("w_done")
        av_done = sem("av_done")
        gate_moved = sem("gate_moved")
        gate_T_done = sem("gate_T_done")
        gate_abs = sem("gate_abs")
        gate_ln = sem("gate_ln")
        gate_m = sem("gate_m")
        gate_em = sem("gate_em")
        gate_back = sem("gate_back")
        gate_cols = sem("gate_cols")
        conv_done = sem("conv_done")
        mqk_ready = sem("mqk_ready")
        s_done = sem("s_done")
        lw_done = sem("lw_done")
        wt_done = sem("wt_done")
        sw_done = sem("sw_done")
        num_done = sem("num_done")
        num_read = sem("num_read")
        msq_done = sem("msq_done")
        mrms_done = sem("mrms_done")
        lssq_done = sem("lssq_done")
        lrms_done = sem("lrms_done")
        angle_done = sem("angle_done")
        trig_done = sem("trig_done")
        lstage_ready = sem("lstage_ready")
        sc_done = sem("sc_done")
        max_done = sem("max_done")
        px_done = sem("px_done")
        pT_done = sem("pT_done")
        pT_read = sem("pT_read")
        lav_done = sem("lav_done")
        dve_chain = sem("dve_chain")
        act_chain = sem("act_chain")
        pool_chain = sem("pool_chain")
        final_done = sem("final_done")
        gainrow_loaded = sem("gainrow_loaded")
        out_stored = sem("out_stored")

        subs, static = [], {}
        pieces, blocks, fills, plains, ffns, sbs, ys = 0, 0, TT * HALVES, 0, 0, 0, 0
        for i in range(DEPTH):
            for part in range(3):
                s = Sub()
                s.index, s.piece0, s.block0, s.fill0, s.plain0, s.y0 = len(subs), pieces, blocks, fills, plains, ys
                if part != 1:
                    s.kind, s.ffn = "ffn", ffns
                    s.wi, s.wo = (ffn1_wi[i], ffn1_wo[i]) if part == 0 else (ffn2_wi[i], ffn2_wo[i])
                    s.gain = (GAIN_FFN1 if part == 0 else GAIN_FFN2) + i * KD
                    s.n_pieces, s.n_blocks, s.n_fills, s.n_plain = 3 * CHUNKS, CHUNKS, CHUNKS + 4, 0
                    ffns += 1
                else:
                    s.kind, j = ("sb", "ml", "mla")[i % 3], i // 3
                    gain = GAIN_MIX + i * KD
                    if s.kind == "sb":
                        cols = [D, 0, D + NCOL, NCOL, 2 * D, 2 * D + NCOL]
                        ps = [rows_piece(sb_w_in[j], 4 * a, 4, c, NCOL, gain + 4 * a) for c in cols for a in range(2)]
                        s.n_blocks, s.n_plain, s.n_fills = 6, 8, 8
                        w_out, head_gain, s.inst = sb_w_out[j], None, sbs
                        sbs += 1
                    elif s.kind == "ml":
                        ps = [rows_piece(ml_w_in[j], 4 * a, 4, b * NCOL, NCOL, gain + 4 * a)
                              for b in range(6) for a in range(2)]
                        ps.insert(1, rows_piece(ml_w_in[j], 0, KD, 3 * D, 2 * ML_HEADS, gain))
                        s.n_blocks, s.n_plain, s.n_fills = 6, 4, 8
                        w_out, head_gain = ml_w_out[j], GAIN_HEAD
                    else:
                        ps = [rows_piece(mla_w_in[j], 4 * a, 4, 0, NCOL, gain + 4 * a) for a in range(2)]
                        ps += [rows_piece(mla_w_in[j], 0, KD, NCOL, MLA_IN - NCOL, gain)]
                        for g in range(MLA_HEADS // GROUP):
                            ps += [rows_piece(mla_w_uq[j], 0, 3, g * GROUP * QK, GROUP * QK, OWN + GAIN_Q),
                                   rows_piece(mla_w_ukv[j], 0, 2, g * NCOL, NCOL, OWN + GAIN_KV)]
                        s.n_blocks, s.n_plain, s.n_fills = 10, 16, 11
                        w_out, head_gain = mla_w_out[j], None
                    s.out0 = pieces + len(ps)
                    ps += [rows_piece(w_out, 2 * a, 2, 0, D, None if head_gain is None else OWN + head_gain + 2 * a)
                           for a in range(4)]
                    s.n_pieces = len(ps)
                    static.update({pieces + n: p for n, p in enumerate(ps)})
                    ys += 4
                pieces += s.n_pieces
                blocks += s.n_blocks
                fills += s.n_fills
                plains += s.n_plain
                s.norm_fill0 = fills - 4
                subs.append(s)
        n_pieces = pieces
        for n, s in enumerate(s for s in subs if s.kind != "ffn"):
            s.pads = n + 1

        def gain_col(g):
            return gains2[:, g - OWN:g - OWN + 1] if g >= OWN else gains1[:, g:g + 1]

        def ffn_piece(s, role, c):
            if role == "C":
                return down_piece(s.wo, c)
            part = "AB".index(role)
            return up_piece(s.wi, c, part, s.gain + 4 * part)

        def piece_at(n):
            s = [s for s in subs if s.piece0 <= n][-1]
            if s.kind != "ffn":
                return static[n]
            m = n - s.piece0
            if m < 2:
                return ffn_piece(s, "AB"[m], 0)
            if m == s.n_pieces - 1:
                return ffn_piece(s, "C", CHUNKS - 1)
            c, r = (m + 1) // 3, (m + 1) % 3
            return ffn_piece(s, "ABC"[r], c if r < 2 else c - 1)

        def load(sp, p, m, c=0):
            slot = m % RING
            if not isinstance(c, int) or m + 3 * c >= RING:
                sp.wait_ge(lo_ready, m + 3 * c - (RING - 1))
            for a, b, ca, cb, src in p.sources:
                dst = raw[:, slot, 0:p.tiles * p.cols].rearrange("p (k n) -> p k n", k=p.tiles)[:, a:b, ca:cb]
                sp.dma_start(dst, src).then_inc(raw_loaded[slot], 16)

        def convert_act(act, p, m, c=0):
            slot = m % RING
            act.wait_ge(raw_loaded[slot], 32 * (m // RING + 1) + 32 * c)
            if not isinstance(c, int) or m + 3 * c >= RING:
                act.wait_ge(piece_used, m + 3 * c - (RING - 1))
            if p.gain is None:
                w = p.tiles * p.cols
                act.activation(whi[:, slot, 0:w], raw[:, slot, 0:w], ACT.Copy).then_inc(hi_ready, 1)
                return
            for k in range(p.tiles):
                r = slice(k * p.cols, (k + 1) * p.cols)
                last = act.activation(whi[:, slot, r], raw[:, slot, r], ACT.Copy, scale=gain_col(p.gain + k))
            last.then_inc(hi_ready, 1)

        def convert_dve(dve, p, m, c=0):
            slot = m % RING
            dve.wait_ge(hi_ready, m + 3 * c + 1)
            hi = whi[:, slot, :].bitcast(F32)
            if p.gain is None:
                w = p.tiles * p.cols
                dve.tensor_tensor(wlo[:, slot, 0:w], raw[:, slot, 0:w], hi[:, 0:w], ALU.subtract).then_inc(lo_ready, 1)
                return
            for k in range(p.tiles):
                r = slice(k * p.cols, (k + 1) * p.cols)
                last = dve.scalar_tensor_tensor(wlo[:, slot, r], raw[:, slot, r], gain_col(p.gain + k), hi[:, r],
                                                op0=ALU.mult, op1=ALU.subtract)
            last.then_inc(lo_ready, 1)

        def converts(eng, convert, *positions):
            for n in positions:
                if n < n_pieces:
                    convert(eng, piece_at(n), n)

        def passes(pe, dst, xh, xl, slot, cols, first, last):
            for n, (a, b) in enumerate(((xh, whi), (xh, wlo), (xl, whi))):
                m = pe.matmul(dst, a, b[:, slot, cols], start=first and n == 0, stop=last and n == 2)
            return m

        def project(pe, slot, t, bank, k0, tiles, cols, first, last):
            for k in range(tiles):
                m = passes(pe, psum[:, bank, 0:cols], xT_hi[:, k0 + k, t * P:(t + 1) * P],
                           xT_lo[:, k0 + k, t * P:(t + 1) * P], slot, slice(k * cols, (k + 1) * cols),
                           first and k == 0, last and k == tiles - 1)
            return m

        def out_group(pe, slot, g, xh, xl, k0, first, last):
            t, nh = GROUPS[g]
            for k in range(2):
                m = passes(pe, psum[:, g, :], xh[:, k0 + k, t * P:(t + 1) * P], xl[:, k0 + k, t * P:(t + 1) * P],
                           slot, slice(k * D + nh * NCOL, k * D + (nh + 1) * NCOL), first and k == 0, last and k == 1)
            return m

        def split_act(act, q, src, dst_hi):
            act.wait_ge(tr_done, q + 1)
            act.activation(dst_hi, src, ACT.Copy).then_inc(tr_hi, 1)

        def split_dve(dve, q, src, dst_hi, dst_lo):
            dve.wait_ge(tr_hi, q + 1)
            dve.tensor_tensor(dst_lo, src, dst_hi.bitcast(F32), ALU.subtract).then_inc(tr_read, 1)

        def fill_pe(pe, src, bank, t, nh):
            for j in range(4):
                m = pe.transpose(psum[:, bank, j * P:(j + 1) * P],
                                 src[:, t, nh * NCOL + j * P:nh * NCOL + (j + 1) * P], ident[:, :])
            m.then_inc(tr_done, 1)

        def fill_split(eng, q, bank, t, k0):
            src = psum[:, bank, :].rearrange("p (j n) -> p j n", j=4)
            hi, lo = (v[:, k0:k0 + 4, t * P:(t + 1) * P] for v in (xT_hi, xT_lo))
            if eng is nc.scalar:
                split_act(eng, q, src, hi)
            else:
                split_dve(eng, q, src, hi, lo)

        def norm_fill0(j):
            return 0 if j == 0 else subs[j - 1].norm_fill0

        def norm_fill(pe, j, g):
            q = norm_fill0(j) + g
            if j:
                pe.wait_ge(h_done, 4 * (j - 1) + g + 1)
            else:
                pe.wait_ge(x_loaded, 16 * TT)
            if q >= 2:
                pe.wait_ge(tr_read, q - 1)
            fill_pe(pe, h, 7 - g % 2, *GROUPS[g])

        def norm_split(eng, j, g):
            t, nh = GROUPS[g]
            fill_split(eng, norm_fill0(j) + g, 7 - g % 2, t, 4 * nh)

        def norm_act(act, j):
            for g in range(4):
                norm_split(act, j, g)
                if j == 0 and g in (1, 2):
                    converts(act, convert_act, g - 1)
                if g >= 2:
                    t = g - 2
                    if j:
                        act.wait_ge(h_done, 4 * (j - 1) + 2 * t + 2)
                    act.activation(y[:, t, :], h[:, t, :], ACT.Square, accum_out=ssq[:, t:t + 1]).then_inc(ssq_done, 1)

        def norm_dve(dve, j, scale):
            def residual(g):
                t, nh = GROUPS[g]
                if g < 3:
                    dve.wait_ge(acc_done, 3 * (j - 1) + g + 1)
                else:
                    dve.wait_ge(piece_used, subs[j - 1].piece0 + subs[j - 1].n_pieces)
                hs = h[:, t, nh * NCOL:(nh + 1) * NCOL]
                dve.scalar_tensor_tensor(hs, psum[:, g, :], scale, hs, op0=ALU.mult, op1=ALU.add).then_inc(h_done, 1)

            if j:
                residual(0)
                residual(1)
                residual(2)
            if j == len(subs):
                residual(3)
                return
            norm_split(dve, j, 0)
            if j:
                residual(3)
            norm_split(dve, j, 1)
            if j == 0:
                converts(dve, convert_dve, 0)
            norm_split(dve, j, 2)
            converts(dve, convert_dve, subs[j].piece0 + 1)
            norm_split(dve, j, 3)

        def first_piece(pe, j):
            s, q = subs[j], norm_fill0(j)
            p = piece_at(s.piece0)
            slot = s.piece0 % RING
            whole = p.tiles == KD
            norm_fill(pe, j, 1)
            norm_fill(pe, j, 2)
            pe.wait_ge(lo_ready, s.piece0 + 1)
            for t in range(TT):
                if t:
                    norm_fill(pe, j, 3)
                pe.wait_ge(tr_read, q + 2 * t + (2 if whole else 1))
                m = project(pe, slot, t, UP[0][t], 0, p.tiles, p.cols, True, whole)
                if whole and t == 0:
                    m.then_inc(proj_done, 1)
            m.then_inc(piece_used, 1)

        def last_piece(pe, s, n, xh, xl, k0):
            j = s.index + 1
            pe.wait_ge(lo_ready, n + 1)
            for g in range(4):
                m = out_group(pe, n % RING, g, xh, xl, k0, False, True)
                m.then_inc(acc_done if g < 3 else piece_used, 1)
                if g == 2 and j < len(subs):
                    norm_fill(pe, j, 0)
            if j < len(subs):
                first_piece(pe, j)

        def ffn_pe(pe, s):
            n0, b0, f0 = s.piece0, s.block0, s.fill0

            def up(m, c, part, banks):
                pe.wait_ge(lo_ready, m + 3 * c + 1)
                for t in range(TT):
                    i = project(pe, m % RING, t, banks[t], 4 * part, 4, 2 * FC, part == 0, part == 1)
                    if part and t == 0:
                        i.then_inc(proj_done, 1)
                i.then_inc(piece_used, 1)

            def hid_fill(c, q):
                pe.wait_ge(proj_read, 2 * (b0 + 1) + 2 * c)
                pe.wait_ge(tr_read, q)
                for b in range(FC // P):
                    for t in range(TT):
                        i = pe.transpose(psum[:, 6, (b * TT + t) * P:(b * TT + t + 1) * P],
                                         hid[:, t, b * P:(b + 1) * P], ident[:, :])
                i.then_inc(tr_done, 1)

            def chunk(c, last=False):
                if not (isinstance(c, int) and c == 1):
                    pe.wait_ge(proj_read, 2 * b0 + 2 * c)
                up(n0 - 1, c, 0, UP[1])
                hid_fill(c - 1, f0 + c - 1)
                up(n0, c, 1, UP[1])
                m = n0 + 1
                pe.wait_ge(lo_ready, m + 3 * c + 1)
                pe.wait_ge(tr_read, f0 + c)
                for g in range(4):
                    i = out_group(pe, m % RING, g, hidT_hi, hidT_lo, 0, isinstance(c, int) and c == 1, False)
                    if last and g == 1:
                        hid_fill(c, f0 + c)
                i.then_inc(piece_used, 1)

            pe.wait_ge(tr_read, norm_fill0(s.index) + 4)
            up(n0 + 1, 0, 1, UP[0])
            chunk(1)
            with pe.Fori(2, CHUNKS - 1) as c:
                chunk(c)
            chunk(CHUNKS - 1, last=True)
            pe.wait_ge(tr_read, f0 + CHUNKS)
            last_piece(pe, s, n0 + 3 * CHUNKS - 1, xT_hi, xT_lo, 0)

        def hidT_views(part):
            return part[:, 0:FC // P, :].rearrange("p b n -> p (b n)")

        def ffn_act(act, s):
            n0, b0 = s.piece0, s.block0

            def gate(c, banks):
                for t in range(TT):
                    if t == 0:
                        act.wait_ge(proj_done, b0 + 1 + c)
                    else:
                        act.wait_ge(piece_used, n0 + 2 if isinstance(c, int) and c == 0 else n0 + 1 + 3 * c)
                    act.activation(silu[:, t, :], psum[:, banks[t], 0:FC], ACT.Silu,
                                   scale=rstd[:, t:t + 1]).then_inc(silu_done, 1)

            def chunk(c, last=False):
                convert_act(act, ffn_piece(s, "C", c - 1), n0 + 1, c)
                split_act(act, s.fill0 + c - 1, psum[:, 6, :], hidT_views(hidT_hi))
                if last:
                    converts(act, convert_act, n0 + 3 * CHUNKS - 1)
                else:
                    convert_act(act, ffn_piece(s, "A", c + 1), n0 + 2, c)
                gate(c, UP[1])
                if last:
                    converts(act, convert_act, n0 + 3 * CHUNKS)
                else:
                    convert_act(act, ffn_piece(s, "B", c + 1), n0 + 3, c)

            converts(act, convert_act, n0 + 2, n0 + 3)
            act.wait_ge(rstd_done, 2 * (s.index + 1))
            gate(0, UP[0])
            chunk(1)
            with act.Fori(2, CHUNKS - 1) as c:
                chunk(c)
            chunk(CHUNKS - 1, last=True)
            split_act(act, s.fill0 + CHUNKS - 1, psum[:, 6, :], hidT_views(xT_hi))
            converts(act, convert_act, n0 + 3 * CHUNKS + 1)

        def ffn_dve(dve, s):
            n0, b0 = s.piece0, s.block0

            def product(c, banks):
                for t in range(TT):
                    dve.wait_ge(silu_done, 2 * CHUNKS * s.ffn + t + 1 + 2 * c)
                    dve.scalar_tensor_tensor(hid[:, t, :], psum[:, banks[t], FC:2 * FC], rstd[:, t:t + 1],
                                             silu[:, t, :], op0=ALU.mult, op1=ALU.mult).then_inc(proj_read, 1)

            def split(c):
                split_dve(dve, s.fill0 + c, psum[:, 6, :], hidT_views(hidT_hi), hidT_views(hidT_lo))

            def chunk(c, last=False):
                convert_dve(dve, ffn_piece(s, "C", c - 1), n0 + 1, c)
                split(c - 1)
                if last:
                    converts(dve, convert_dve, n0 + 3 * CHUNKS - 1)
                else:
                    convert_dve(dve, ffn_piece(s, "A", c + 1), n0 + 2, c)
                product(c, UP[1])
                if last:
                    split_dve(dve, s.fill0 + c, psum[:, 6, :], hidT_views(xT_hi), hidT_views(xT_lo))
                    converts(dve, convert_dve, n0 + 3 * CHUNKS)
                else:
                    convert_dve(dve, ffn_piece(s, "B", c + 1), n0 + 3, c)

            converts(dve, convert_dve, n0 + 2, n0 + 3)
            dve.wait_ge(rstd_done, 2 * (s.index + 1))
            product(0, UP[0])
            chunk(1)
            with dve.Fori(2, CHUNKS - 1) as c:
                chunk(c)
            chunk(CHUNKS - 1, last=True)

        def pair(b):
            return UP[1 if b else 0]

        def block_wait(eng, s, b, t, last):
            if t == 0:
                eng.wait_ge(proj_done, s.block0 + b + 1)
            else:
                eng.wait_ge(piece_used, s.piece0 + last + 1)

        def block_piece(pe, s, b, n, k0, first, last, between=None):
            m = s.piece0 + n
            p = piece_at(m)
            pe.wait_ge(lo_ready, m + 1)
            for t in range(TT):
                if first and b >= 2:
                    pe.wait_ge(proj_read, 2 * (s.block0 + b) - 1 + t)
                i = project(pe, m % RING, t, pair(b)[t], k0, p.tiles, p.cols, first, last)
                if last and t == 0:
                    i.then_inc(proj_done, 1)
                if t == 0 and between:
                    between()
            i.then_inc(piece_used, 1)

        def plain_fill(pe, s, f, bank, blocks_in, width):
            if f >= 2:
                pe.wait_ge(plain_read, s.plain0 + f - 1)
            for j, b in enumerate(blocks_in):
                i = pe.transpose(psum[0:width, bank, j * P:(j + 1) * P], b, ident[:, :])
            i.then_inc(plain_T, 1)

        def y_fill(pe, s, g, bank):
            pe.wait_ge(y_ready, s.y0 + g + 1)
            if g:
                pe.wait_ge(tr_read, s.norm_fill0 - 4 + g)
            for k in range(2):
                for t in range(TT):
                    i = pe.transpose(psum[:, bank, (k * TT + t) * P:(k * TT + t + 1) * P],
                                     y[:, t, (2 * g + k) * P:(2 * g + k + 1) * P], ident[:, :])
            i.then_inc(tr_done, 1)

        def y_split(eng, s, g, bank):
            hi, lo = (v[:, 2 * g:2 * g + 2, :].rearrange("p k n -> p (k n)") for v in (xT_hi, xT_lo))
            if eng is nc.scalar:
                split_act(eng, s.norm_fill0 - 4 + g, psum[:, bank, :], hi)
            else:
                split_dve(eng, s.norm_fill0 - 4 + g, psum[:, bank, :], hi, lo)

        def out_piece(pe, s, a, between={}):
            pe.wait_ge(tr_read, s.norm_fill0 - 4 + a + 1)
            if a == 3:
                last_piece(pe, s, s.out0 + 3, xT_hi, xT_lo, 6)
                return
            pe.wait_ge(lo_ready, s.out0 + a + 1)
            for g in range(4):
                i = out_group(pe, (s.out0 + a) % RING, g, xT_hi, xT_lo, 2 * a, a == 0, False)
                if g in between:
                    between[g]()
            i.then_inc(piece_used, 1)

        def evacuate(dve, s, b, last, dst, scale=None):
            for t in range(TT):
                block_wait(dve, s, b, t, last)
                src = psum[:, pair(b)[t], 0:dst.shape[2]]
                if scale is None:
                    i = dve.tensor_scalar(dst[:, t, :], src, rstd[:, t:t + 1], None, ALU.mult)
                else:
                    i = dve.tensor_scalar(dst[:, t, :], src, rstd[:, t:t + 1], scale, ALU.mult, ALU.mult)
                i.then_inc(proj_read, 1)

        def scores_pe(pe, g, bank, k_even, k_odd, q, start):
            for hh in range(GROUP):
                pair, k = 2 * g + hh // 2, (k_even, k_odd)[hh % 2]
                pe.matmul(psum[:, bank + hh // 2, hh % 2 * SEQ:(hh % 2 + 1) * SEQ], k[:, pair, 0:P], q[:, pair, :],
                          start=start and hh % 2 == 0, stop=hh % 2 == 1, skip_group_check=True)
            for hh in range(GROUP):
                pair, k = 2 * g + hh // 2, (k_even, k_odd)[hh % 2]
                i = pe.matmul(psum[:, bank + 2, hh * P:(hh + 1) * P], k[:, pair, P:SEQ], q[:, pair, P:SEQ],
                              start=start and hh == 0, stop=hh == 3, skip_group_check=True)
            return i

        def mask_pe(pe, m, bank):
            for b in range(3):
                pe.matmul(psum[:, bank + b, :], ident_b[:, :], mask[:, 2 * m + b // 2, :], start=True, stop=False,
                          skip_group_check=True)

        def banks3(bank):
            return psum[:, bank:bank + 3, :].rearrange("p b n -> p (b n)")

        def magnitude(dve, dst, src):
            return dve.tensor_scalar(dst.bitcast(I32), src.bitcast(I32), 0x7FFFFFFF, None, ALU.bitwise_and)

        SB_Z, SB_AV = (0, 0, 0, 4), (3, 7, 7, 7)

        def sb_pe(pe, s):
            def transposes(b):
                pe.wait_ge(proj_read, 2 * (s.block0 + b + 1))
                for t in range(TT):
                    plain_fill(pe, s, 2 * b + t, 6 + t, [stage[:, t, j * P:(j + 1) * P] for j in range(4)], P)

            def scores(g):
                pe.wait_ge(plain_read, s.plain0 + (4 if g < 2 else 8))
                if g == 0:
                    pe.wait_ge(pad_ready, s.pads)
                if g == 3:
                    pe.wait_ge(proj_read, 2 * (s.block0 + 6))
                elif g:
                    pe.wait_ge(w_done, 4 * s.inst + g)
                mask_pe(pe, 0, SB_Z[g])
                scores_pe(pe, g, SB_Z[g], kT_even, kT_odd, qT, False).then_inc(z_done, 1)

            def remainder(g):
                bank, sp3 = SB_Z[g], sb_sp[:, g % 2, :]
                pe.wait_ge(sp_done, 4 * s.inst + g + 1)
                for b in range(3):
                    pe.matmul(psum[:, bank + b, :], neg_tri[:, :], sp3[:, b * NCOL:(b + 1) * NCOL], start=False,
                              stop=b == 2, skip_group_check=True)
                for b in range(2):
                    i = pe.matmul(psum[:, bank + b, :].rearrange("p (a n) -> p a n", a=2)[:, :, P:SEQ], neg_ones[:, :],
                                  sp3[:, 2 * NCOL + b * SEQ:2 * NCOL + (b + 1) * SEQ].rearrange("p (a n) -> p a n", a=2),
                                  start=False, stop=True, skip_group_check=True)
                i.then_inc(r_done, 1)

            def values(g):
                w3 = sb_e[:, g % 2, :]
                pe.wait_ge(w_done, 4 * s.inst + g + 1)
                if g >= 2:
                    pe.wait_ge(tr_read, s.norm_fill0 - 4 + g)
                pe.wait_ge(proj_read, 2 * (s.block0 + (5 if g < 2 else 6)))
                for t in range(TT):
                    for hh in range(GROUP):
                        c = (GROUP * g + hh) * 64
                        dst = psum[:, SB_AV[g], (t * GROUP + hh) * 64:(t * GROUP + hh + 1) * 64]
                        i = pe.matmul(dst, w3[:, hh * SEQ + t * P:hh * SEQ + (t + 1) * P], v_sb[:, 0, c:c + 64],
                                      start=t == 0 and hh == 0, stop=t == 0, skip_group_check=True)
                        if t:
                            i = pe.matmul(dst, w3[:, 2 * NCOL + hh * P:2 * NCOL + (hh + 1) * P], v_sb[:, 1, c:c + 64],
                                          start=False, stop=True, skip_group_check=True)
                i.then_inc(av_done, 1)

            def piece(n):
                block_piece(pe, s, n // 2, n, 4 * (n % 2), n % 2 == 0, n % 2 == 1)

            pe.wait_ge(tr_read, norm_fill0(s.index) + 4)
            piece(1)
            piece(2)
            transposes(0)
            piece(3)
            piece(4)
            transposes(1)
            piece(5)
            scores(0)
            piece(6)
            transposes(2)
            piece(7)
            remainder(0)
            piece(8)
            transposes(3)
            scores(1)
            piece(9)
            piece(10)
            remainder(1)
            values(0)
            scores(2)
            values(1)
            piece(11)
            y_fill(pe, s, 0, 3)
            y_fill(pe, s, 1, 7)
            remainder(2)
            scores(3)
            pe.wait_ge(w_done, 4 * s.inst + 3)
            out_piece(pe, s, 0)
            values(2)
            remainder(3)
            y_fill(pe, s, 2, 7)
            out_piece(pe, s, 1)
            values(3)
            out_piece(pe, s, 2, {1: lambda: y_fill(pe, s, 3, 7)})
            out_piece(pe, s, 3)

        def sb_act(act, s, link):
            def copies(b):
                pairs = slice(0, 4) if b < 2 else slice(4, 8)
                for t in range(TT):
                    act.wait_ge(plain_T, s.plain0 + 2 * b + t + 1)
                    bank, cols = psum[:, 6 + t, :].rearrange("p (j n) -> p j n", j=4), slice(t * P, (t + 1) * P)
                    if b % 2 == 0:
                        act.activation(kT_even[0:64, pairs, cols], bank[0:64, :, :], ACT.Copy)
                        i = act.activation(kT_odd[64:P, pairs, cols], bank[64:P, :, :], ACT.Copy)
                    else:
                        i = act.activation(qT[:, pairs, cols], bank, ACT.Copy)
                    i.then_inc(plain_read, 1)

            def log1p(g):
                e = sb_e[:, g % 2, :]
                act.wait_ge(abs_done, 4 * s.inst + g + 1)
                act.activation(e, e, ACT.Exp, scale=-1.0).then_inc(exp_done, 1)
                act.wait_ge(exp_done, 4 * s.inst + g + 1)
                act.activation(e, e, ACT.Ln, bias=1.0).then_inc(ln_done, 1)

            def weights(g):
                act.wait_ge(r_done, 4 * s.inst + g + 1)
                act.activation(sb_e[:, g % 2, :], banks3(SB_Z[g]), ACT.Exp).then_inc(w_done, 1)

            def conv(n):
                converts(act, convert_act, s.piece0 + n)

            for n in (2, 3, 4):
                conv(n)
            act.preload_act_table_set("natural_log_exp_and_others")
            act.wait_ge(pad_ready, s.pads)
            copies(0)
            conv(5)
            conv(6)
            copies(1)
            conv(7)
            conv(8)
            log1p(0)
            copies(2)
            conv(9)
            weights(0)
            conv(10)
            copies(3)
            conv(11)
            log1p(1)
            conv(12)
            weights(1)
            conv(13)
            log1p(2)
            y_split(act, s, 0, 3)
            y_split(act, s, 1, 7)
            conv(14)
            weights(2)
            log1p(3)
            conv(15)
            weights(3)
            y_split(act, s, 2, 7)
            conv(16)
            y_split(act, s, 3, 7)
            conv(17)

        def sb_dve(dve, s, link):
            def evac(b):
                dst = stage if b < 4 else v_sb[:, :, (b - 4) * NCOL:(b - 3) * NCOL]
                evacuate(dve, s, b, 2 * b + 1, dst, SB_SCALE if b in (1, 3) else None)

            def absolute(g):
                dve.wait_ge(z_done, 4 * s.inst + g + 1)
                magnitude(dve, sb_e[:, g % 2, :], banks3(SB_Z[g])).then_inc(abs_done, 1)

            def softplus(g):
                dve.wait_ge(ln_done, 4 * s.inst + g + 1)
                dve.scalar_tensor_tensor(sb_sp[:, g % 2, :], banks3(SB_Z[g]), 0.0, sb_e[:, g % 2, :],
                                         op0=ALU.max, op1=ALU.add).then_inc(sp_done, 1)

            def heads(g):
                dve.wait_ge(av_done, 4 * s.inst + g + 1)
                dve.tensor_copy(y[:, :, g * SEQ:(g + 1) * SEQ],
                                psum[:, SB_AV[g], :].rearrange("p (t n) -> p t n", t=TT)).then_inc(y_ready, 1)

            def conv(n):
                converts(dve, convert_dve, s.piece0 + n)

            conv(2)
            conv(3)
            dve.wait_ge(rstd_done, 2 * (s.index + 1))
            evac(0)
            conv(4)
            conv(5)
            evac(1)
            conv(6)
            conv(7)
            evac(2)
            absolute(0)
            conv(8)
            softplus(0)
            conv(9)
            evac(3)
            conv(10)
            absolute(1)
            conv(11)
            evac(4)
            softplus(1)
            conv(12)
            heads(0)
            absolute(2)
            conv(13)
            heads(1)
            softplus(2)
            evac(5)
            y_split(dve, s, 0, 3)
            y_split(dve, s, 1, 7)
            conv(14)
            absolute(3)
            softplus(3)
            conv(15)
            heads(2)
            y_split(dve, s, 2, 7)
            heads(3)
            conv(16)
            y_split(dve, s, 3, 7)

        def sb_set_up(pool, link):
            pool.memset(kT_even, 0.0)
            pool.memset(kT_odd, 0.0).then_inc(pad_ready, 1)

        def ml_pe(pe, s):
            def piece(n, between=None):
                b = (n - 1) // 2
                block_piece(pe, s, b, n, 4 * ((n + 1) % 2), n % 2 == 1, n % 2 == 0, between)

            def gates():
                m = s.piece0 + 1
                pe.wait_ge(lo_ready, m + 1)
                for k in range(KD):
                    cols = slice(k * 2 * ML_HEADS, (k + 1) * 2 * ML_HEADS)
                    for n, (w, v) in enumerate(((whi, xT_hi), (wlo, xT_hi), (whi, xT_lo))):
                        i = pe.matmul(psum[0:2 * ML_HEADS, 3, 0:SEQ], w[:, m % RING, cols], v[:, k, :],
                                      start=k == 0 and n == 0, stop=k == KD - 1 and n == 2)
                i.then_inc(piece_used, 1)

            def gates_token_major():
                pe.wait_ge(gate_moved, 1)
                for t in range(TT):
                    i = pe.transpose(psum[:, 3, t * 2 * ML_HEADS:(t + 1) * 2 * ML_HEADS],
                                     gate_raw[0:2 * ML_HEADS, t * P:(t + 1) * P], ident[0:2 * ML_HEADS, 0:2 * ML_HEADS])
                i.then_inc(gate_T_done, 1)

            def gates_T():
                pe.wait_ge(gate_moved, 2)
                for c in range(2):
                    for t in range(TT):
                        i = pe.transpose(psum[0:ML_HEADS, 3, (c * TT + t) * P:(c * TT + t + 1) * P],
                                         gate_in[:, t, c * ML_HEADS:(c + 1) * ML_HEADS], ident[:, :])
                i.then_inc(gate_T_done, 1)

            def gates_back():
                pe.wait_ge(gate_em, 1)
                for c, rows in enumerate((g_a, g_em)):
                    for t in range(TT):
                        i = pe.transpose(psum[:, 3, (c * TT + t) * ML_HEADS:(c * TT + t + 1) * ML_HEADS],
                                         rows[:, t * P:(t + 1) * P], ident[0:ML_HEADS, 0:ML_HEADS])
                i.then_inc(gate_back, 1)

            def transposes(part):
                pe.wait_ge(proj_read, 2 * (s.block0 + part + 1))
                for t in range(TT):
                    plain_fill(pe, s, 2 * part + t, 6 + t, [stage[:, t, j * P:(j + 1) * P] for j in range(4)], P)

            def log_weights(g):
                if g:
                    pe.wait_ge(sw_done, g)
                mask_pe(pe, 1, 0)
                for hh in range(GROUP):
                    pe.matmul(psum[:, hh // 2, hh % 2 * SEQ:(hh % 2 + 1) * SEQ], sel[:, GROUP * g + hh, :], g_M,
                              start=False, stop=hh % 2 == 1, skip_group_check=True)
                for hh in range(GROUP):
                    i = pe.matmul(psum[:, 2, hh * P:(hh + 1) * P], sel[:, GROUP * g + hh, :], g_M[:, P:SEQ],
                                  start=False, stop=hh == 3, skip_group_check=True)
                i.then_inc(lw_done, 1)

            def scores(g):
                pe.wait_ge(mqk_ready, 2)
                pe.wait_ge(wt_done, g + 1)
                scores_pe(pe, g, 0, mkT_even, mkT_odd, mqT, True).then_inc(s_done, 1)

            def numerators(g):
                pe.wait_ge(proj_read, 2 * (s.block0 + 3 + g))
                pe.wait_ge(plain_read, s.plain0 + 4)
                if g:
                    pe.wait_ge(num_read, g)
                pe.wait_ge(sw_done, g + 1)
                for t in range(TT):
                    for hh in range(GROUP):
                        c = (GROUP * g + hh) * P
                        parts = [(ml_sw[:, hh * SEQ + t * P:hh * SEQ + (t + 1) * P], 0)]
                        if t:
                            parts.append((ml_sw[:, 2 * NCOL + hh * P:2 * NCOL + (hh + 1) * P], 1))
                        for n, (w, kt) in enumerate(parts):
                            pe.matmul(psum[:, 6 + t, hh * P:(hh + 1) * P], w, mv[:, kt, c:c + P],
                                      start=hh == 0 and n == 0, stop=n == t, skip_group_check=True)
                        for n, (w, kt) in enumerate(parts):
                            i = pe.matmul(psum[:, 3, t * GROUP + hh:t * GROUP + hh + 1], w, ones[:, 0:1],
                                          start=t == 0 and hh == 0 and n == 0, stop=n == t, skip_group_check=True)
                i.then_inc(num_done, 1)

            pe.wait_ge(tr_read, norm_fill0(s.index) + 4)
            gates()
            piece(2)
            gates_token_major()
            piece(3, lambda: transposes(0))
            gates_T()
            piece(4)
            piece(5, lambda: transposes(1))
            piece(6)
            gates_back()
            log_weights(0)
            piece(7)
            piece(8)
            scores(0)
            piece(9)
            numerators(0)
            log_weights(1)
            piece(10)
            scores(1)
            piece(11)
            numerators(1)
            piece(12)
            pe.wait_ge(num_read, 2)
            y_fill(pe, s, 0, 6)
            out_piece(pe, s, 0, {1: lambda: y_fill(pe, s, 1, 7)})
            out_piece(pe, s, 1, {1: lambda: y_fill(pe, s, 2, 6)})
            out_piece(pe, s, 2, {1: lambda: y_fill(pe, s, 3, 7)})
            out_piece(pe, s, 3)

        def ml_act(act, s, link):
            def conv(n):
                converts(act, convert_act, s.piece0 + n)

            def copies(part):
                for t in range(TT):
                    act.wait_ge(plain_T, s.plain0 + 2 * part + t + 1)
                    act.activation(conv_in[part][:, :, 3 + t * P:3 + (t + 1) * P],
                                   psum[:, 6 + t, :].rearrange("p (j n) -> p j n", j=4), ACT.Copy).then_inc(plain_read, 1)

            def exps(g):
                act.wait_ge(lw_done, g + 1)
                if g:
                    act.wait_ge(sw_done, g)
                for hh in range(GROUP):
                    head, c = GROUP * g + hh, hh * SEQ
                    act.activation(ml_wt[:, c:c + SEQ], psum[:, hh // 2, hh % 2 * SEQ:(hh % 2 + 1) * SEQ], ACT.Exp,
                                   bias=gate_T[:, 0, head:head + 1])
                for hh in range(GROUP):
                    head, c = GROUP * g + hh, 2 * NCOL + hh * P
                    i = act.activation(ml_wt[:, c:c + P], psum[:, 2, hh * P:(hh + 1) * P], ACT.Exp,
                                       bias=gate_T[:, 1, head:head + 1])
                i.then_inc(wt_done, 1)

            def output_gate(half):
                for t in range(TT):
                    block_wait(act, s, 4 + half, t, 10 + 2 * half)
                    act.activation(mo[:, t, half * NCOL:(half + 1) * NCOL], psum[:, pair(4)[t], :], ACT.Sigmoid,
                                   scale=rstd[:, t:t + 1]).then_inc(proj_read, 1)

            def squares(g):
                act.wait_ge(num_read, g + 1)
                for t in range(TT):
                    for hh in range(GROUP):
                        c, m = (GROUP * g + hh) * P, t * GROUP + hh
                        i = act.activation(stage[:, t, hh * P:(hh + 1) * P], y[:, t, c:c + P], ACT.Square,
                                           accum_out=mssq[:, g, m:m + 1])
                i.then_inc(msq_done, 1)

            for n in (2, 3, 4, 5):
                conv(n)
            act.wait_ge(pad_ready, s.pads)
            copies(0)
            conv(6)
            act.preload_act_table_set("natural_log_exp_and_others")
            act.wait_ge(gate_abs, 1)
            link(act.activation(g_t, g_t, ACT.Exp, scale=-1.0))
            act.activation(g_t, g_t, ACT.Ln, bias=1.0).then_inc(gate_ln, 1)
            conv(7)
            copies(1)
            act.wait_ge(gate_m, 1)
            act.activation(g_em, g_t, ACT.Exp, scale=-1.0).then_inc(gate_em, 1)
            conv(8)
            act.wait_ge(conv_done, 1)
            act.activation(mqT, q_out, ACT.Silu).then_inc(mqk_ready, 1)
            conv(9)
            act.wait_ge(gate_cols, 1)
            act.wait_ge(mqk_ready, 1)
            exps(0)
            conv(10)
            act.wait_ge(conv_done, 2)
            act.activation(mkT_even[0:64, :, :], k_out[0:64, :, :], ACT.Silu)
            act.activation(mkT_odd[64:P, :, :], k_out[64:P, :, :], ACT.Silu).then_inc(mqk_ready, 1)
            conv(11)
            conv(12)
            exps(1)
            squares(0)
            output_gate(0)
            conv(13)
            conv(14)
            squares(1)
            output_gate(1)
            y_split(act, s, 0, 6)
            conv(15)
            y_split(act, s, 1, 7)
            conv(16)
            y_split(act, s, 2, 6)
            conv(17)
            y_split(act, s, 3, 7)
            conv(18)

        def ml_dve(dve, s, link):
            def conv(n):
                converts(dve, convert_dve, s.piece0 + n)

            def evac(b, dst):
                evacuate(dve, s, b, 2 * b + 2, dst)

            def convolve(part, tiles):
                dve.wait_ge(plain_read, s.plain0 + 2 * (part + 1))
                src, dst = conv_in[part], conv_out[part]
                for j in (3, 2, 1, 0):
                    for k in tiles:
                        w = CONV_W + j * KD + 4 * part + k
                        if j == 3:
                            i = dve.tensor_scalar(dst[:, k, :], src[:, k, 3:3 + SEQ], gains2[:, w:w + 1], None, ALU.mult)
                        else:
                            i = dve.scalar_tensor_tensor(dst[:, k, :], src[:, k, j:j + SEQ], gains2[:, w:w + 1],
                                                         dst[:, k, :], op0=ALU.mult, op1=ALU.add)
                    if j:
                        link(i)
                if tiles[-1] == 3:
                    i.then_inc(conv_done, 1)

            def weigh(g):
                dve.wait_ge(s_done, g + 1)
                dve.wait_ge(wt_done, g + 1)
                if g:
                    dve.wait_ge(num_done, g)
                dve.scalar_tensor_tensor(ml_sw, banks3(0), ML_SCALE, ml_wt, op0=ALU.mult,
                                         op1=ALU.mult).then_inc(sw_done, 1)

            def outputs(g):
                dve.wait_ge(num_done, g + 1)
                link(magnitude(dve, den, psum[:, 3, 0:TT * GROUP].rearrange("p (t h) -> p t h", t=TT)))
                link(dve.tensor_tensor(den, den, gate_T[:, 2:4, GROUP * g:GROUP * (g + 1)], ALU.max))
                link(dve.reciprocal(den, den))
                for t in range(TT):
                    i = dve.tensor_tensor(y[:, t, g * NCOL:(g + 1) * NCOL].rearrange("p (h v) -> p h v", h=GROUP),
                                          psum[:, 6 + t, :].rearrange("p (h v) -> p h v", h=GROUP),
                                          den[:, t, :].unsqueeze(2).broadcast_to((P, GROUP, P)), ALU.mult)
                i.then_inc(num_read, 1)

            def gated(g):
                dve.wait_ge(mrms_done, g + 1)
                dve.wait_ge(proj_read, 2 * (s.block0 + 5 + g))
                for hh in range(GROUP):
                    c = slice((GROUP * g + hh) * P, (GROUP * g + hh + 1) * P)
                    for t in range(TT):
                        m = t * GROUP + hh
                        i = dve.scalar_tensor_tensor(y[:, t, c], y[:, t, c], mrms[:, g, m:m + 1], mo[:, t, c],
                                                     op0=ALU.mult, op1=ALU.mult)
                    if hh % 2:
                        i.then_inc(y_ready, 1)

            conv(2)
            conv(3)
            dve.wait_ge(piece_used, s.piece0 + 2)
            dve.tensor_copy(gate_raw[0:2 * ML_HEADS, :], psum[0:2 * ML_HEADS, 3, 0:SEQ]).then_inc(gate_moved, 1)
            conv(4)
            dve.wait_ge(rstd_done, 2 * (s.index + 1))
            evac(0, stage)
            dve.wait_ge(gate_T_done, 1)
            for t in range(TT):
                i = dve.tensor_scalar(gate_in[:, t, :], psum[:, 3, t * 2 * ML_HEADS:(t + 1) * 2 * ML_HEADS],
                                      rstd[:, t:t + 1], None, ALU.mult)
            i.then_inc(gate_moved, 1)
            conv(5)
            convolve(0, (0, 1))
            dve.wait_ge(pad_ready, s.pads)
            dve.wait_ge(gate_T_done, 2)
            dve.tensor_scalar(g_i, psum[0:ML_HEADS, 3, 0:SEQ], gate_bias[:, 0:1], None, ALU.add)
            link(dve.tensor_scalar(g_f, psum[0:ML_HEADS, 3, SEQ:2 * SEQ], gate_bias[:, 1:2], None, ALU.add))
            dve.tensor_scalar(g_min, g_f, 0.0, None, ALU.min)
            magnitude(dve, g_t, g_f).then_inc(gate_abs, 1)
            conv(6)
            evac(1, stage)
            dve.wait_ge(gate_ln, 1)
            link(dve.tensor_tensor(g_f, g_min, g_t, ALU.subtract))
            link(dve.tensor_tensor_scan(g_F, g_one, g_f, 0.0, ALU.mult, ALU.add))
            link(dve.tensor_tensor(g_a, g_i, g_F, ALU.subtract))
            link(dve.tensor_tensor_scan(g_M[0:ML_HEADS, :], g_a, g_a, 0.0, ALU.max, ALU.max))
            dve.tensor_tensor(g_t, g_F, g_M[0:ML_HEADS, :], ALU.add).then_inc(gate_m, 1)
            conv(7)
            convolve(0, (2, 3))
            conv(8)
            convolve(1, (0, 1))
            evac(2, mv[:, :, 0:NCOL])
            dve.wait_ge(gate_back, 1)
            dve.tensor_copy(gate_T, psum[:, 3, 0:4 * ML_HEADS].rearrange("p (c h) -> p c h", c=4)).then_inc(gate_cols, 1)
            conv(9)
            convolve(1, (2, 3))
            conv(10)
            evac(3, mv[:, :, NCOL:D])
            weigh(0)
            conv(11)
            dve.wait_ge(gate_cols, 1)
            outputs(0)
            conv(12)
            weigh(1)
            conv(13)
            gated(0)
            conv(14)
            outputs(1)
            y_split(dve, s, 0, 6)
            gated(1)
            conv(15)
            y_split(dve, s, 1, 7)
            conv(16)
            y_split(dve, s, 2, 6)
            conv(17)
            y_split(dve, s, 3, 7)

        def ml_set_up(pool, link):
            pool.memset(q_in[:, :, 0:3], 0.0)
            pool.memset(k_in[:, :, 0:3], 0.0)
            pool.memset(mkT_even, 0.0)
            pool.memset(mkT_odd, 0.0)
            pool.memset(g_M, 0.0)
            pool.memset(g_one, 1.0)
            link(pool.memset(sel, 0.0))
            pool.affine_select(out=sel, in_=sel, compare_op=ALU.not_equal, fill=-1.0, base=0,
                               pattern=[[-1, ML_HEADS], [0, P]], channel_multiplier=1).then_inc(pad_ready, 1)

        def ml_pool(pool, link):
            for g in range(2):
                pool.wait_ge(msq_done, g + 1)
                link(pool.tensor_scalar(mssq[:, g, :], mssq[:, g, :], 1.0 / P, EPS, ALU.mult, ALU.add))
                pool.tensor_tensor(mrms[:, g, :], mssq[:, g, :], minus_half[:, 0:TT * GROUP],
                                   ALU.pow).then_inc(mrms_done, 1)

        LT_SC, LT_AV = (0, 0, 4, 4), (3, 3, 7, 7)

        def latent_split(eng, s, f):
            bank = psum[:, 6 + f % 2, :]
            if f < 2:
                src = bank[:, 0:3 * P].rearrange("p (k n) -> p k n", k=3)
                hi, lo = (v[:, 0:3, f * P:(f + 1) * P] for v in (xT_hi, xT_lo))
            else:
                src = bank
                hi, lo = (v[:, 3:5, :].rearrange("p k n -> p (k n)") for v in (xT_hi, xT_lo))
            if eng is nc.scalar:
                split_act(eng, s.fill0 + f, src, hi)
            else:
                split_dve(eng, s.fill0 + f, src, hi, lo)

        def lt_pe(pe, s):
            def latent_fill(f):
                if f < 2:
                    pe.wait_ge(proj_read, 2 * s.block0 + f + 1)
                else:
                    pe.wait_ge(proj_read, 2 * (s.block0 + 2))
                    pe.wait_ge(tr_read, s.fill0 + 1)
                for j, (k, t) in enumerate([(k, f) for k in range(3)] if f < 2 else [(k, t) for k in (3, 4) for t in range(TT)]):
                    i = pe.transpose(psum[:, 6 + f % 2, j * P:(j + 1) * P], lc[:, t, k * P:(k + 1) * P], ident[:, :])
                i.then_inc(tr_done, 1)

            def q_block(g):
                block_piece(pe, s, 2 + 2 * g, 3 + 2 * g, 0, True, True)

            def kv_block(g):
                block_piece(pe, s, 3 + 2 * g, 4 + 2 * g, 3, True, True)

            def transposes_q(g):
                pe.wait_ge(lstage_ready, g + 1)
                for t in range(TT):
                    plain_fill(pe, s, 4 * g + t, 6 + t, [lq[:, t * GROUP + hh, :] for hh in range(GROUP)], QK)

            def transposes_k(g):
                pe.wait_ge(proj_read, 2 * (s.block0 + 4 + 2 * g))
                for t in range(TT):
                    plain_fill(pe, s, 4 * g + 2 + t, 6 + t, [lk[:, t * GROUP + hh, :] for hh in range(GROUP)], QK)

            def scores(g):
                bank = LT_SC[g]
                pe.wait_ge(plain_read, s.plain0 + 4 * (g + 1))
                if g == 2:
                    pe.wait_ge(plain_read, s.plain0 + 16)
                    pe.wait_ge(proj_read, 2 * (s.block0 + 10))
                elif g:
                    pe.wait_ge(pT_read, g)
                mask_pe(pe, 2, bank)
                for hh in range(GROUP):
                    n = GROUP * g + hh
                    pe.matmul(psum[:, bank + hh // 2, hh % 2 * SEQ:(hh % 2 + 1) * SEQ], lqT[0:QK, n, P:SEQ],
                              lkT[0:QK, n, :], start=False, stop=hh % 2 == 1, skip_group_check=True)
                for hh in range(GROUP):
                    n = GROUP * g + hh
                    i = pe.matmul(psum[:, bank + 2, hh * P:(hh + 1) * P], lqT[0:QK, n, 0:P], lkT[0:QK, n, 0:P],
                                  start=False, stop=hh == 3, skip_group_check=True)
                i.then_inc(sc_done, 1)

            def transposes_p(g):
                pe.wait_ge(px_done, g + 1)
                for n, (start, step) in enumerate(((0, SEQ), (P, SEQ), (2 * NCOL, P))):
                    for hh in range(GROUP):
                        c = start + hh * step
                        i = pe.transpose(psum[:, LT_SC[g] + n, hh * P:(hh + 1) * P], l_px[:, c:c + P], ident[:, :])
                i.then_inc(pT_done, 1)

            def values(g):
                pe.wait_ge(pT_read, g + 1)
                if g:
                    pe.wait_ge(tr_read, s.norm_fill0 - 4 + g)
                for t in range(TT):
                    for hh in range(GROUP):
                        c = (GROUP * g + hh) * VD
                        dst = psum[:, LT_AV[g], (t * GROUP + hh) * VD:(t * GROUP + hh + 1) * VD]
                        parts = [(2, 0)] if t == 0 else [(0, 0), (1, 1)]
                        for n, (part, kt) in enumerate(parts):
                            i = pe.matmul(dst, l_pT[:, part * NCOL + hh * P:part * NCOL + (hh + 1) * P],
                                          lv[:, kt, c:c + VD], start=t == 0 and hh == 0, stop=n == t,
                                          skip_group_check=True)
                i.then_inc(lav_done, 1)

            pe.wait_ge(tr_read, norm_fill0(s.index) + 4)
            block_piece(pe, s, 0, 1, 4, False, True)
            block_piece(pe, s, 1, 2, 0, True, True, lambda: latent_fill(0))
            latent_fill(1)
            latent_fill(2)
            pe.wait_ge(tr_read, s.fill0 + 2)
            q_block(0)
            pe.wait_ge(tr_read, s.fill0 + 3)
            kv_block(0)
            transposes_q(0)
            q_block(1)
            transposes_k(0)
            kv_block(1)
            scores(0)
            transposes_q(1)
            q_block(2)
            transposes_k(1)
            kv_block(2)
            transposes_p(0)
            transposes_q(2)
            q_block(3)
            scores(1)
            transposes_k(2)
            values(0)
            kv_block(3)
            transposes_q(3)
            transposes_p(1)
            y_fill(pe, s, 0, 3)
            transposes_k(3)
            values(1)
            scores(2)
            y_fill(pe, s, 1, 7)
            pe.wait_ge(pT_read, 2)
            out_piece(pe, s, 0, {1: lambda: transposes_p(2)})
            scores(3)
            values(2)
            out_piece(pe, s, 1, {1: lambda: y_fill(pe, s, 2, 7)})
            transposes_p(3)
            out_piece(pe, s, 2, {0: lambda: values(3), 2: lambda: y_fill(pe, s, 3, 7)})
            out_piece(pe, s, 3)

        def lt_act(act, s, link):
            def conv(n):
                converts(act, convert_act, s.piece0 + n)

            def squares(n, a, b):
                for t in range(TT):
                    scratch = l_pT[:, TT * a + t * (b - a):TT * a + (t + 1) * (b - a)]
                    i = act.activation(scratch, lc[:, t, a:b], ACT.Square, accum_out=lssq[:, n, t:t + 1])
                return i

            def copies(f, dst, g):
                for t in range(TT):
                    act.wait_ge(plain_T, s.plain0 + f + t + 1)
                    act.activation(dst[0:QK, GROUP * g:GROUP * (g + 1), t * P:(t + 1) * P],
                                   psum[0:QK, 6 + t, :].rearrange("p (j n) -> p j n", j=4), ACT.Copy).then_inc(plain_read, 1)

            def copies_q(g):
                copies(4 * g, lqT, g)

            def copies_k(g):
                copies(4 * g + 2, lkT, g)

            def exps(g):
                act.wait_ge(max_done, g + 1)
                if g:
                    act.wait_ge(pT_done, g)
                if g >= 2:
                    act.wait_ge(y_ready, s.y0 + g - 1)
                for t, n, c0 in ((1, SEQ, 0), (0, P, 2 * NCOL)):
                    for hh in range(GROUP):
                        m, c = 4 * (1 - t) + hh, c0 + hh * n
                        i = act.activation(l_px[:, c:c + n], banks3(LT_SC[g])[:, c:c + n], ACT.Exp, bias=lneg[:, m:m + 1],
                                           accum_out=lsum[:, g % 2, m:m + 1])
                i.then_inc(px_done, 1)

            def copy_p(g):
                act.wait_ge(pT_done, g + 1)
                if g:
                    act.wait_ge(lav_done, g)
                act.activation(l_pT, banks3(LT_SC[g]), ACT.Copy).then_inc(pT_read, 1)

            conv(2)
            conv(3)
            act.wait_ge(angle_done, 1)
            act.activation(trig, angle, ACT.Sin).then_inc(trig_done, 1)
            conv(4)
            act.wait_ge(proj_read, 2 * (s.block0 + 1))
            squares(0, 0, Q_RANK)
            latent_split(act, s, 0)
            latent_split(act, s, 1)
            latent_split(act, s, 2)
            act.wait_ge(proj_read, 2 * (s.block0 + 2))
            squares(1, Q_RANK, Q_RANK + KV_RANK).then_inc(lssq_done, 1)
            conv(5)
            conv(6)
            copies_q(0)
            conv(7)
            copies_k(0)
            conv(8)
            copies_q(1)
            conv(9)
            exps(0)
            copies_k(1)
            conv(10)
            copy_p(0)
            copies_q(2)
            conv(11)
            copies_k(2)
            conv(12)
            exps(1)
            copies_q(3)
            copy_p(1)
            y_split(act, s, 0, 3)
            copies_k(3)
            conv(13)
            exps(2)
            y_split(act, s, 1, 7)
            copy_p(2)
            conv(14)
            exps(3)
            y_split(act, s, 2, 7)
            copy_p(3)
            conv(15)
            y_split(act, s, 3, 7)
            conv(16)

        def lt_dve(dve, s, link):
            def conv(n):
                converts(dve, convert_dve, s.piece0 + n)

            def rope(x1, x2, o1, o2, tmp, sin, cos):
                dve.tensor_tensor(tmp[0], x1, cos, ALU.mult)
                dve.tensor_tensor(tmp[1], x2, sin, ALU.mult)
                dve.tensor_tensor(tmp[2], x1, sin, ALU.mult)
                link(dve.tensor_tensor(tmp[3], x2, cos, ALU.mult))
                dve.tensor_tensor(o1, tmp[0], tmp[1], ALU.subtract)
                return dve.tensor_tensor(o2, tmp[2], tmp[3], ALU.add)

            def tile(t):
                return psum[:, pair(2)[t], :], slice(t * GROUP, (t + 1) * GROUP)

            def read_q(g):
                b = 2 + 2 * g
                if g:
                    dve.wait_ge(plain_T, s.plain0 + 4 * g - 2)
                for t in range(TT):
                    block_wait(dve, s, b, t, b + 1)
                    bank, hs = tile(t)
                    dve.tensor_scalar(lq[:, hs, :], bank[:, 0:GROUP * QK].rearrange("p (h d) -> p h d", h=GROUP),
                                      lrms[:, 0, t:t + 1], MLA_SCALE, ALU.mult, ALU.mult).then_inc(proj_read, 1)
                dve.wait_ge(proj_read, 2 * (s.block0 + b + 1))
                for t in range(TT):
                    q4 = lq[:, tile(t)[1], :]
                    x1, x2 = q4[:, :, NOPE:NOPE + HALF], q4[:, :, NOPE + HALF:QK]
                    sn, cs = (v[:, t, :].unsqueeze(1).broadcast_to((P, GROUP, HALF)) for v in (sin, cos))
                    i = rope(x1, x2, x1, x2, [rope_tmp[:, n, tile(t)[1], :] for n in range(4)], sn, cs)
                i.then_inc(lstage_ready, 1)

            def read_kv(g):
                b = 3 + 2 * g
                if g:
                    dve.wait_ge(plain_T, s.plain0 + 4 * g)
                for t in range(TT):
                    block_wait(dve, s, b, t, b + 1)
                    bank, hs = tile(t)
                    kv = bank.rearrange("p (h d) -> p h d", h=GROUP)
                    dve.tensor_scalar(lk[:, hs, 0:NOPE], kv[:, :, 0:NOPE], lrms[:, 1, t:t + 1], None, ALU.mult)
                    dve.tensor_scalar(lv[:, t, g * SEQ:(g + 1) * SEQ].rearrange("p (h d) -> p h d", h=GROUP),
                                      kv[:, :, NOPE:NOPE + VD], lrms[:, 1, t:t + 1], None, ALU.mult).then_inc(proj_read, 1)

            def maxima(g):
                dve.wait_ge(sc_done, g + 1)
                bank = LT_SC[g]
                dve.tensor_reduce(lmax[:, 0:4], psum[:, bank:bank + 2, :].rearrange("p b (h n) -> p (b h) n", h=2), AX,
                                  ALU.max)
                link(dve.tensor_reduce(lmax[:, 4:8], psum[:, bank + 2, :].rearrange("p (h n) -> p h n", h=4), AX, ALU.max))
                if g:
                    dve.wait_ge(px_done, g)
                dve.tensor_scalar(lneg, lmax, -1.0, None, ALU.mult).then_inc(max_done, 1)

            def heads(g):
                dve.wait_ge(px_done, g + 1)
                if g:
                    dve.wait_ge(y_ready, s.y0 + g)
                link(dve.reciprocal(linv, lsum[:, g % 2, :]))
                dve.wait_ge(lav_done, g + 1)
                for t in range(TT):
                    i = dve.tensor_tensor(y[:, t, g * SEQ:(g + 1) * SEQ].rearrange("p (h v) -> p h v", h=GROUP),
                                          psum[:, LT_AV[g], t * SEQ:(t + 1) * SEQ].rearrange("p (h v) -> p h v", h=GROUP),
                                          linv[:, 4 - 4 * t:8 - 4 * t].unsqueeze(2).broadcast_to((P, GROUP, VD)), ALU.mult)
                i.then_inc(y_ready, 1)

            conv(2)
            conv(3)
            dve.wait_ge(pad_ready, s.pads)
            link(dve.tensor_copy(pos_f, pos_i[:, :]))
            for n in range(4):
                i = dve.tensor_scalar(angle[:, n, :], inv_freq, pos_f[:, n % TT:n % TT + 1], None, ALU.mult)
            link(i)
            for n in range(4):
                i = dve.tensor_scalar(turns[:, n, :], angle[:, n, :], 1.0 / TWO_PI, 0.25 * (n // TT), ALU.mult, ALU.add)
            link(i)
            link(dve.tensor_scalar(turns, turns, ROUND, None, ALU.add))
            link(dve.tensor_scalar(turns, turns, ROUND, None, ALU.subtract))
            for part in TWO_PI_PARTS:
                link(dve.scalar_tensor_tensor(angle, turns, -part, angle, op0=ALU.mult, op1=ALU.add))
            link(dve.tensor_scalar(angle[:, TT:4, :], angle[:, TT:4, :], TWO_PI / 4, None, ALU.add))
            dve.tensor_scalar(angle, angle, -SIN_MAX, SIN_MAX, ALU.max, ALU.min).then_inc(angle_done, 1)
            dve.wait_ge(rstd_done, 2 * (s.index + 1))
            evacuate(dve, s, 0, 1, lc[:, :, 0:NCOL])
            conv(4)
            latent_split(dve, s, 0)
            evacuate(dve, s, 1, 2, lc[:, :, NCOL:MLA_IN])
            latent_split(dve, s, 1)
            latent_split(dve, s, 2)
            dve.wait_ge(trig_done, 1)
            dve.wait_ge(proj_read, 2 * (s.block0 + 2))
            kr_in = lc[:, :, Q_RANK + KV_RANK:MLA_IN]
            sin, cos = trig[:, 0:TT, :], trig[:, TT:4, :]
            link(rope(kr_in[:, :, 0:HALF], kr_in[:, :, HALF:ROPE], kr[:, :, 0:HALF], kr[:, :, HALF:ROPE],
                      [rope_tmp[:, n, 0:TT, :] for n in range(4)], sin, cos))
            for t in range(TT):
                dve.tensor_copy(lk[:, t * GROUP:(t + 1) * GROUP, NOPE:QK],
                                kr[:, t, :].unsqueeze(1).broadcast_to((P, GROUP, ROPE)))
            conv(5)
            dve.wait_ge(lrms_done, 1)
            read_q(0)
            conv(6)
            read_kv(0)
            conv(7)
            read_q(1)
            conv(8)
            read_kv(1)
            maxima(0)
            conv(9)
            read_q(2)
            conv(10)
            read_kv(2)
            conv(11)
            read_q(3)
            maxima(1)
            conv(12)
            heads(0)
            read_kv(3)
            y_split(dve, s, 0, 3)
            heads(1)
            maxima(2)
            conv(13)
            y_split(dve, s, 1, 7)
            maxima(3)
            heads(2)
            conv(14)
            y_split(dve, s, 2, 7)
            conv(15)
            heads(3)
            y_split(dve, s, 3, 7)

        def lt_set_up(pool, link):
            for j in range(HALF):
                i = pool.memset(inv_freq[:, j:j + 1], ROPE_THETA ** (-j / HALF))
            i.then_inc(pad_ready, 1)

        def lt_pool(pool, link):
            pool.wait_ge(lssq_done, 1)
            for n, rank in enumerate((Q_RANK, KV_RANK)):
                i = pool.tensor_scalar(lms[:, n, :], lssq[:, n, :], 1.0 / rank, EPS, ALU.mult, ALU.add)
            link(i)
            pool.tensor_tensor(lrms.rearrange("p n t -> p (n t)"), lms.rearrange("p n t -> p (n t)"), minus_half[:, 0:4],
                               ALU.pow).then_inc(lrms_done, 1)

        MIXERS = {"sb": {"set_up": sb_set_up, "pe": sb_pe, "act": sb_act, "dve": sb_dve},
                  "ml": {"set_up": ml_set_up, "pe": ml_pe, "act": ml_act, "dve": ml_dve, "pool": ml_pool},
                  "mla": {"set_up": lt_set_up, "pe": lt_pe, "act": lt_act, "dve": lt_dve, "pool": lt_pool}}

        block = ctx.enter_context(nc.Block())

        @block.sync
        def _(sp):
            for a, g in enumerate((ln_ffn1, ln_mix, ln_ffn2)):
                sp.dma_start(stage[a * DEPTH * KD:(a + 1) * DEPTH * KD, 0, 0:P],
                             g.rearrange("l (k p) -> (l k) p", p=P)).then_inc(gains_loaded, 16)
            for t in range(TT):
                sp.dma_start(h[:, t, :], x[0, t * P:(t + 1) * P, :]).then_inc(x_loaded, 16)
            for s in subs:
                end = s.piece0 + s.n_pieces
                if s.kind != "ffn":
                    for n in range(s.piece0, end):
                        load(sp, piece_at(n), n)
                    continue
                for n in range(s.piece0, s.piece0 + 5):
                    load(sp, piece_at(n), n)
                with sp.Fori(2, CHUNKS) as c:
                    for r, role in enumerate("ABC"):
                        load(sp, ffn_piece(s, role, c if r < 2 else c - 1), s.piece0 - 1 + r, c)
                load(sp, piece_at(end - 1), end - 1)
            sp.dma_start(gain_row, ln_final.rearrange("(a n) -> a n", a=1).broadcast_to((P, D))).then_inc(gainrow_loaded, 16)
            for t in range(TT):
                sp.wait_ge(final_done, t + 1)
                sp.dma_start(out[0, t * P:(t + 1) * P, :], y[:, t, :]).then_inc(out_stored, 16)
            sp.wait_ge(out_stored, 16 * TT)

        @block.gpsimd
        def _(pool):
            chain = [0]

            def link(ins):
                chain[0] += 1
                ins.then_inc(pool_chain, 1)
                pool.wait_ge(pool_chain, chain[0])

            link(pool.memset(ident[:, :], 0.0))
            pool.affine_select(out=ident[:, :], in_=ident[:, :], compare_op=ALU.not_equal, fill=1.0, base=0,
                               pattern=[[-1, P]], channel_multiplier=1).then_inc(const_done, 1)
            pool.wait_ge(const_done, 1)
            pool.memset(minus_half[:, :], -0.5)
            pool.memset(ones[:, :], 1.0)
            pool.memset(neg_ones[:, :], -1.0)
            link(pool.memset(neg_tri[:, :], -1.0))
            link(pool.affine_select(out=neg_tri[:, :], in_=neg_tri[:, :], compare_op=ALU.is_ge, fill=0.0, base=0,
                                    pattern=[[-1, P]], channel_multiplier=1))
            link(pool.tensor_copy(ident_b[:, :], ident[:, :]))
            link(pool.memset(mask[:, :, :], 0.0))
            for m, (base, mult, step) in enumerate(((0, -1, 1), (1, -1, 1), (1, 1, -1))):
                blocks4 = mask[:, 2 * m + 1, :].rearrange("p (a n) -> p a n", a=4)
                blocks2 = mask[:, 2 * m, :].rearrange("p (a b n) -> p a b n", a=2, b=2)
                for view in ([blocks4, blocks2[:, :, 1 if m == 2 else 0, :]]):
                    last = pool.affine_select(out=view, in_=view, compare_op=ALU.is_gt, fill=NEG, base=base,
                                              pattern=[[0, view.shape[1]], [step, P]], channel_multiplier=mult)
            last.then_inc(const_done, 1)
            for j in range(len(subs) + 1):
                if j < len(subs) and subs[j].kind != "ffn":
                    MIXERS[subs[j].kind]["set_up"](pool, link)
                for t in range(TT):
                    pool.wait_ge(ssq_done, TT * j + t + 1)
                    link(pool.tensor_scalar(mean_sq[:, t:t + 1], ssq[:, t:t + 1], 1.0 / D, EPS, ALU.mult, ALU.add))
                    pool.tensor_tensor(rstd[:, t:t + 1], mean_sq[:, t:t + 1], minus_half[:, 0:1],
                                       ALU.pow).then_inc(rstd_done, 1)
                if j < len(subs) and "pool" in MIXERS.get(subs[j].kind, {}):
                    MIXERS[subs[j].kind]["pool"](pool, link)

        @block.scalar
        def _(act):
            chain = [0]

            def act_link(ins):
                chain[0] += 1
                ins.then_inc(act_chain, 1)
                act.wait_ge(act_chain, chain[0])

            for at, n, v in ((GAIN_Q, 3, mla_g_q), (GAIN_KV, 2, mla_g_kv)):
                act.dma_start(stage[at:at + n, 1, 0:P], v[0, :].rearrange("(k p) -> k p", p=P)).then_inc(par_loaded, 16)
            act.dma_start(stage[GAIN_HEAD:GAIN_HEAD + KD, 1, 0:P], ml_head_gain[0, :, :]).then_inc(par_loaded, 16)
            act.dma_start(stage[CONV_W:CONV_W + 4 * KD, 1, 0:P],
                          ml_conv_w[0, :, :].rearrange("j (k p) -> (j k) p", p=P)).then_inc(par_loaded, 16)
            for col, b in enumerate((ml_b_igate, ml_b_fgate)):
                act.dma_start(gate_bias[:, col:col + 1], b[0, :].rearrange("(h a) -> h a", a=1)).then_inc(par_loaded, 16)
            act.dma_start(pos_i[:, :], positions[0, :].rearrange("(t p) -> p t", p=P),
                          allow_slow_non_contiguous=True).then_inc(par_loaded, 16)
            act.preload_act_table_set("natural_log_exp_and_others")
            act.wait_ge(x_loaded, 16 * TT)
            act.wait_ge(gains_ready, 1)
            norm_act(act, 0)
            for s in subs:
                if s.kind == "ffn":
                    ffn_act(act, s)
                else:
                    MIXERS[s.kind]["act"](act, s, act_link)
                if s.index + 1 < len(subs):
                    norm_act(act, s.index + 1)
            for t in range(TT):
                act.wait_ge(h_done, 4 * len(subs) - 2 + 2 * t)
                act.activation(y[:, t, :], h[:, t, :], ACT.Square, accum_out=ssq[:, t:t + 1]).then_inc(ssq_done, 1)

        @block.vector
        def _(dve):
            chain = [0]

            def link(ins):
                chain[0] += 1
                ins.then_inc(dve_chain, 1)
                dve.wait_ge(dve_chain, chain[0])

            dve.wait_ge(par_T, 1)
            dve.tensor_copy(gains1[:, :], psum[:, 0, 0:N_GAINS_1]).then_inc(gains_ready, 1)
            dve.wait_ge(gains_ready, 1)
            norm_dve(dve, 0, None)
            dve.wait_ge(par_T, 2)
            dve.tensor_copy(gains2[:, :], psum[:, 2, 0:N_GAINS_2]).then_inc(gains_ready, 1)
            for s in subs:
                if s.kind == "ffn":
                    ffn_dve(dve, s)
                else:
                    MIXERS[s.kind]["dve"](dve, s, link)
                norm_dve(dve, s.index + 1, 0.5 if s.kind == "ffn" else 1.0)
            dve.wait_ge(gainrow_loaded, 16)
            for t in range(TT):
                dve.wait_ge(rstd_done, TT * len(subs) + t + 1)
                dve.scalar_tensor_tensor(y[:, t, :], h[:, t, :], rstd[:, t:t + 1], gain_row, op0=ALU.mult,
                                         op1=ALU.mult).then_inc(final_done, 1)

        @block.tensor
        def _(pe):
            pe.wait_ge(const_done, 1)
            pe.wait_ge(gains_loaded, 16 * 3)
            pe.transpose(psum[:, 0, 0:N_GAINS_1], stage[0:N_GAINS_1, 0, 0:P],
                         ident[0:N_GAINS_1, 0:N_GAINS_1]).then_inc(par_T, 1)
            norm_fill(pe, 0, 0)
            pe.wait_ge(gains_ready, 1)
            first_piece(pe, 0)
            pe.wait_ge(par_loaded, 16 * 7)
            pe.transpose(psum[:, 2, 0:N_GAINS_2], stage[0:N_GAINS_2, 1, 0:P],
                         ident[0:N_GAINS_2, 0:N_GAINS_2]).then_inc(par_T, 1)
            pe.wait_ge(const_done, 2)
            for s in subs:
                if s.kind == "ffn":
                    ffn_pe(pe, s)
                else:
                    MIXERS[s.kind]["pe"](pe, s)


NAMES = ["x", "positions", "ln_ffn1", "ffn1_wi", "ffn1_wo", "ln_mix", "ln_ffn2", "ffn2_wi", "ffn2_wo",
         "sb_w_in", "sb_w_out", "ml_w_in", "ml_conv_w", "ml_b_igate", "ml_b_fgate", "ml_head_gain", "ml_w_out",
         "mla_w_in", "mla_g_q", "mla_w_uq", "mla_g_kv", "mla_w_ukv", "mla_w_out", "ln_final"]


def kernel(**inputs):
    import numpy as np
    import concourse.bacc as bacc
    from concourse.bass_utils import run_bass_kernel_spmd

    nc = bacc.Bacc("TRN2", target_bir_lowering=False, num_devices=1)
    arrays, args = {}, []
    for name in NAMES:
        a = np.ascontiguousarray(inputs[name])
        arrays[f"in_{name}"] = a
        args.append(nc.dram_tensor(f"in_{name}", a.shape, mybir.dt.from_np(a.dtype), kind="ExternalInput").ap())
    args.append(nc.dram_tensor("out_0", (1, SEQ, D), F32, kind="ExternalOutput").ap())
    trunk(nc, *args)
    r = run_bass_kernel_spmd(nc, [arrays], core_ids=[0])
    return r.results[0]["out_0"]
```
